# Optimizing a Trainium2 kernel written in Bass

```python
import math
import jax, jax.numpy as jnp
from jax import lax
import numpy as np

D_MODEL = 1024
BATCH = 1
SEQ = 256
DEPTH = 2
DEC_BATCH = 8
DEC_SEQ = 8
PAST_LEN = 2048
PAGE_SIZE = 128

N_META = 16
SSD_EXPAND = 2
D_INNER = SSD_EXPAND * D_MODEL
HEAD_DIM = 64
N_HEADS = D_INNER // HEAD_DIM
N_GROUPS = 4
D_STATE = 128
CONV_K = 4
CONV_DIM = D_INNER + 2 * N_GROUPS * D_STATE
CHUNK = 128
POOL_WINDOWS = (2, 4, 8, 16)
N_POOL_GROUPS = 4
POOL_DIM = D_MODEL
POOL_GROUP_DIM = POOL_DIM // N_POOL_GROUPS
MAX_WIN = 16
D_FF = ((8 * D_MODEL // 3 + 127) // 128) * 128
IN_COLS = D_INNER + CONV_DIM + N_HEADS + POOL_DIM + 2 * D_MODEL
EPS = 1e-6

kernel_name = 'hybrid_ssd_pool_macaron_decode_step'

def rmsnorm(x, g):
    xf = x.astype(jnp.float32)
    out = xf * lax.rsqrt(jnp.mean(xf * xf, axis=-1, keepdims=True) + EPS) * g.astype(jnp.float32)
    return out.astype(x.dtype)

def swiglu(h, w_in, w_out):
    gate, up = jnp.split(h @ w_in, 2, axis=-1)
    return (jax.nn.silu(gate) * up) @ w_out

def depthwise_causal_conv(full, w, b):
    c = full.shape[-1]
    out = lax.conv_general_dilated(full, w[:, None, :].astype(full.dtype), window_strides=(1,), padding='VALID',
                                   dimension_numbers=('NWC', 'WIO', 'NWC'), feature_group_count=c)
    return out + b.astype(full.dtype)

def ssd_scan(xh, dt, a_neg, bm, cm, init, front, chunk):
    b, t, h, p = xh.shape
    g, n = bm.shape[2], bm.shape[3]
    r = h // g
    back = (-(front + t)) % chunk

    def pad(v):
        return jnp.pad(v, [(0, 0), (front, back)] + [(0, 0)] * (v.ndim - 2))

    xh, dt, bm, cm = pad(xh), pad(dt), pad(bm), pad(cm)
    nc = (front + t + back) // chunk
    xc = xh.reshape(b, nc, chunk, g, r, p)
    dtc = dt.reshape(b, nc, chunk, g, r)
    bc = bm.reshape(b, nc, chunk, g, n)
    cc = cm.reshape(b, nc, chunk, g, n)
    acum = jnp.cumsum(dtc * a_neg.reshape(g, r), axis=2)
    xdt = xc * dtc[..., None]
    causal = jnp.tril(jnp.ones((chunk, chunk), dtype=bool))[:, :, None, None]
    seg = acum[:, :, :, None] - acum[:, :, None, :]
    lmat = jnp.exp(jnp.where(causal, seg, -jnp.inf))
    cb = jnp.einsum('bcign,bcjgn->bcijg', cc, bc)
    y_intra = jnp.einsum('bcijgr,bcjgrp->bcigrp', cb[..., None] * lmat, xdt)
    decay_end = jnp.exp(acum[:, :, -1:] - acum)
    cs = jnp.einsum('bcjgn,bcjgrp->bcgrpn', bc, xdt * decay_end[..., None])
    chunk_decay = jnp.exp(acum[:, :, -1])

    def step(s, inp):
        cs_c, d_c = inp
        return s * d_c[..., None, None] + cs_c, s

    final, prev = lax.scan(step, init.reshape(b, g, r, p, n),
                           (jnp.moveaxis(cs, 1, 0), jnp.moveaxis(chunk_decay, 1, 0)))
    prev = jnp.moveaxis(prev, 0, 1)
    y_inter = jnp.einsum('bcign,bcgrpn->bcigrp', cc, prev) * jnp.exp(acum)[..., None]
    y = (y_intra + y_inter).reshape(b, nc * chunk, h, p)[:, front:front + t]
    return y, final.reshape(b, h, p, n)

def multiscale_pool(u, buf, pos0, w_grp, scale):
    b, t, _ = u.shape
    pw = MAX_WIN - 1
    full = jnp.concatenate([buf.astype(u.dtype), u], axis=1)
    csum = jnp.cumsum(jnp.pad(full.astype(jnp.float32), ((0, 0), (1, 0), (0, 0))), axis=1)
    pos = pos0 + jnp.arange(t)
    means = []
    for k, w in enumerate(POOL_WINDOWS):
        lo, hi = k * POOL_GROUP_DIM, (k + 1) * POOL_GROUP_DIM
        s = csum[:, pw + 1:pw + 1 + t, lo:hi] - csum[:, pw + 1 - w:pw + 1 - w + t, lo:hi]
        cnt = jnp.minimum(pos + 1, w).astype(jnp.float32)
        means.append(s / cnt[None, :, None])
    pooled = jnp.stack(means, axis=2) - u.astype(jnp.float32).reshape(b, t, N_POOL_GROUPS, POOL_GROUP_DIM)
    mixed = jnp.einsum('btgc,gcd->btgd', pooled.astype(u.dtype), w_grp).reshape(b, t, POOL_DIM) * scale
    return mixed, full[:, -pw:]

def mixer(h, ssm0, conv0, pool0, pos0, front, chunk, prm, l):
    b, t, _ = h.shape
    f32 = jnp.float32
    proj = h @ prm['w_in'][l]
    o1 = D_INNER
    o2 = o1 + CONV_DIM
    o3 = o2 + N_HEADS
    o4 = o3 + POOL_DIM
    o5 = o4 + D_MODEL
    z, xbc, dt_raw = proj[..., :o1], proj[..., o1:o2], proj[..., o2:o3]
    u, g_ssd, g_pool = proj[..., o3:o4], proj[..., o4:o5], proj[..., o5:]
    full = jnp.concatenate([conv0.astype(xbc.dtype), xbc], axis=1)
    xbc = jax.nn.silu(depthwise_causal_conv(full, prm['conv_w'][l], prm['conv_b'][l]))
    new_conv = full[:, -(CONV_K - 1):]
    gn = N_GROUPS * D_STATE
    xs = xbc[..., :D_INNER].reshape(b, t, N_HEADS, HEAD_DIM).astype(f32)
    bm = xbc[..., D_INNER:D_INNER + gn].reshape(b, t, N_GROUPS, D_STATE).astype(f32)
    cm = xbc[..., D_INNER + gn:].reshape(b, t, N_GROUPS, D_STATE).astype(f32)
    dt = jax.nn.softplus(dt_raw.astype(f32) + prm['dt_bias'][l].astype(f32))
    a_neg = -jnp.exp(prm['a_log'][l].astype(f32))
    y, new_ssm = ssd_scan(xs, dt, a_neg, bm, cm, ssm0.astype(f32), front, chunk)
    y = y + prm['d_skip'][l].astype(f32)[:, None] * xs
    y = y.reshape(b, t, D_INNER).astype(h.dtype)
    y = rmsnorm(y * jax.nn.silu(z), prm['ssd_norm'][l])
    ssd_out = y @ prm['w_ssd_branch'][l]
    pooled, new_pool = multiscale_pool(u, pool0, pos0, prm['pool_w'][l], prm['pool_scale'][l])
    pool_out = pooled @ prm['w_pool_branch'][l]
    merged = jax.nn.sigmoid(g_ssd) * ssd_out + jax.nn.sigmoid(g_pool) * pool_out
    return merged @ prm['w_out'][l], new_ssm.astype(h.dtype), new_conv, new_pool

def run_trunk(x, ssm, conv, pool, pos0, front, chunk, prm):
    new_ssm, new_conv, new_pool = [], [], []
    for l in range(DEPTH):
        f = swiglu(rmsnorm(x, prm['ln_ffn1_pre'][l]), prm['ffn1_w_in'][l], prm['ffn1_w_out'][l])
        x = x + 0.5 * rmsnorm(f, prm['ln_ffn1_post'][l])
        m, s, c, p = mixer(rmsnorm(x, prm['ln_mix_pre'][l]), ssm[l], conv[l], pool[l], pos0, front, chunk, prm, l)
        x = x + rmsnorm(m, prm['ln_mix_post'][l])
        f = swiglu(rmsnorm(x, prm['ln_ffn2_pre'][l]), prm['ffn2_w_in'][l], prm['ffn2_w_out'][l])
        x = x + 0.5 * rmsnorm(f, prm['ln_ffn2_post'][l])
        new_ssm.append(s)
        new_conv.append(c)
        new_pool.append(p)
    return x, jnp.stack(new_ssm), jnp.stack(new_conv), jnp.stack(new_pool)

def setup_inputs(seed: int = 0) -> dict:
    key = jax.random.key(seed)
    ks = iter(jax.random.split(key, 40))
    f32 = jnp.float32

    def nrm(shape, scale):
        return jax.random.normal(next(ks), shape, f32) * scale

    def gain(width):
        return 1.0 + nrm((DEPTH, width), 0.05)

    x_prompt = nrm((BATCH, SEQ, D_MODEL), 1.0)
    x_sample = nrm((DEC_BATCH, DEC_SEQ, D_MODEL), 1.0)
    state_ssm = nrm((DEPTH, DEC_BATCH, N_HEADS, HEAD_DIM, D_STATE), 0.1)
    state_conv = nrm((DEPTH, DEC_BATCH, CONV_K - 1, CONV_DIM), 1.0)
    state_pool = nrm((DEPTH, DEC_BATCH, MAX_WIN - 1, POOL_DIM), 1.0)
    meta_tokens = nrm((N_META, D_MODEL), 1.0)
    ln_ffn1_pre = gain(D_MODEL)
    ln_ffn1_post = gain(D_MODEL)
    ffn1_w_in = nrm((DEPTH, D_MODEL, 2 * D_FF), D_MODEL ** -0.5)
    ffn1_w_out = nrm((DEPTH, D_FF, D_MODEL), D_FF ** -0.5)
    ln_mix_pre = gain(D_MODEL)
    ln_mix_post = gain(D_MODEL)
    w_in = nrm((DEPTH, D_MODEL, IN_COLS), D_MODEL ** -0.5)
    conv_w = nrm((DEPTH, CONV_K, CONV_DIM), CONV_K ** -0.5)
    conv_b = nrm((DEPTH, CONV_DIM), 0.02)
    dt0 = jnp.exp(jax.random.uniform(next(ks), (DEPTH, N_HEADS), f32, math.log(1e-3), math.log(1e-1)))
    dt_bias = dt0 + jnp.log(-jnp.expm1(-dt0))
    a_log = jnp.log(jax.random.uniform(next(ks), (DEPTH, N_HEADS), f32, 1.0, 16.0))
    d_skip = 1.0 + nrm((DEPTH, N_HEADS), 0.1)
    ssd_norm = gain(D_INNER)
    w_ssd_branch = nrm((DEPTH, D_INNER, D_MODEL), D_INNER ** -0.5)
    pool_w = nrm((DEPTH, N_POOL_GROUPS, POOL_GROUP_DIM, POOL_GROUP_DIM), POOL_GROUP_DIM ** -0.5)
    pool_scale = gain(POOL_DIM)
    w_pool_branch = nrm((DEPTH, POOL_DIM, D_MODEL), POOL_DIM ** -0.5)
    w_out = nrm((DEPTH, D_MODEL, D_MODEL), D_MODEL ** -0.5)
    ln_ffn2_pre = gain(D_MODEL)
    ln_ffn2_post = gain(D_MODEL)
    ffn2_w_in = nrm((DEPTH, D_MODEL, 2 * D_FF), D_MODEL ** -0.5)
    ffn2_w_out = nrm((DEPTH, D_FF, D_MODEL), D_FF ** -0.5)
    return {'x_prompt': x_prompt, 'x_sample': x_sample, 'state_ssm': state_ssm, 'state_conv': state_conv,
            'state_pool': state_pool, 'meta_tokens': meta_tokens, 'ln_ffn1_pre': ln_ffn1_pre,
            'ln_ffn1_post': ln_ffn1_post, 'ffn1_w_in': ffn1_w_in, 'ffn1_w_out': ffn1_w_out,
            'ln_mix_pre': ln_mix_pre, 'ln_mix_post': ln_mix_post, 'w_in': w_in, 'conv_w': conv_w,
            'conv_b': conv_b, 'dt_bias': dt_bias, 'a_log': a_log, 'd_skip': d_skip, 'ssd_norm': ssd_norm,
            'w_ssd_branch': w_ssd_branch, 'pool_w': pool_w, 'pool_scale': pool_scale,
            'w_pool_branch': w_pool_branch, 'w_out': w_out, 'ln_ffn2_pre': ln_ffn2_pre,
            'ln_ffn2_post': ln_ffn2_post, 'ffn2_w_in': ffn2_w_in, 'ffn2_w_out': ffn2_w_out}

def reference(x_prompt, x_sample, state_ssm, state_conv, state_pool, meta_tokens, ln_ffn1_pre, ln_ffn1_post,
              ffn1_w_in, ffn1_w_out, ln_mix_pre, ln_mix_post, w_in, conv_w, conv_b, dt_bias, a_log, d_skip,
              ssd_norm, w_ssd_branch, pool_w, pool_scale, w_pool_branch, w_out, ln_ffn2_pre, ln_ffn2_post,
              ffn2_w_in, ffn2_w_out):
    prm = dict(ln_ffn1_pre=ln_ffn1_pre, ln_ffn1_post=ln_ffn1_post, ffn1_w_in=ffn1_w_in, ffn1_w_out=ffn1_w_out,
               ln_mix_pre=ln_mix_pre, ln_mix_post=ln_mix_post, w_in=w_in, conv_w=conv_w, conv_b=conv_b,
               dt_bias=dt_bias, a_log=a_log, d_skip=d_skip, ssd_norm=ssd_norm, w_ssd_branch=w_ssd_branch,
               pool_w=pool_w, pool_scale=pool_scale, w_pool_branch=w_pool_branch, w_out=w_out,
               ln_ffn2_pre=ln_ffn2_pre, ln_ffn2_post=ln_ffn2_post, ffn2_w_in=ffn2_w_in, ffn2_w_out=ffn2_w_out)
    bp = x_prompt.shape[0]
    dtype = x_prompt.dtype
    meta = jnp.broadcast_to(meta_tokens.astype(dtype)[None], (bp, N_META, D_MODEL))
    xp = jnp.concatenate([meta, x_prompt], axis=1)
    ssm_z = jnp.zeros((DEPTH, bp, N_HEADS, HEAD_DIM, D_STATE), dtype)
    conv_z = jnp.zeros((DEPTH, bp, CONV_K - 1, CONV_DIM), dtype)
    pool_z = jnp.zeros((DEPTH, bp, MAX_WIN - 1, POOL_DIM), dtype)
    front = (-N_META) % CHUNK
    yp, ssm_p, conv_p, pool_p = run_trunk(xp, ssm_z, conv_z, pool_z, 0, front, CHUNK, prm)
    y_prompt = yp[:, N_META:]
    sample_chunk = min(CHUNK, x_sample.shape[1])
    y_sample, ssm_s, conv_s, pool_s = run_trunk(x_sample, state_ssm, state_conv, state_pool, PAST_LEN, 0,
                                                sample_chunk, prm)
    return (y_prompt, y_sample, ssm_p, conv_p, pool_p, ssm_s, conv_s, pool_s)


_drawn_inputs = setup_inputs


def setup_inputs(seed=0):
    import zlib

    import numpy as np

    out = dict(_drawn_inputs(seed))
    spreads = {}
    factors = {}
    for name, (base, spread) in spreads.items():
        noise = np.random.default_rng([zlib.crc32(name.encode()), seed]).standard_normal(out[name].shape)
        drawn = base * np.exp(spread * noise) if base else spread * noise
        out[name] = __import__('jax').numpy.asarray(drawn.astype(out[name].dtype))
    for name, factor in factors.items():
        out[name] = (out[name] * factor).astype(out[name].dtype)
    return out
```

```python
from contextlib import ExitStack

import concourse.bass as bass
from concourse import mybir
from concourse.alu_op_type import AluOpType as ALU

ACT = mybir.ActivationFunctionType
F32 = mybir.dt.float32
F32R = mybir.dt.float32r

P = 128
D_MODEL, D_FF, D_INNER, DEPTH = 1024, 2816, 2048, 2
N_HEADS, HEAD_DIM, N_GROUPS, D_STATE = 32, 64, 4, 128
SEQS, STEPS, N_META, SEQ = 8, 8, 16, 256
CONV_K, MAX_WIN = 4, 16
EPS = 1e-6

KD, KF, KI = D_MODEL // P, D_FF // P, D_INNER // P
SAMPLE = SEQS * STEPS
T = SAMPLE + N_META + SEQ
CHUNKS = [(0, SAMPLE + N_META), (SAMPLE + N_META, P), (SAMPLE + N_META + P, P)]
NXBC = KI + 2 * N_GROUPS
HIST = CONV_K - 1
CSTRIDE = STEPS + HIST
CW = SEQS * CSTRIDE + HIST + N_META + SEQ
CP = SEQS * CSTRIDE
PHIST = MAX_WIN - 1
PSTRIDE = STEPS + PHIST
PW = SEQS * PSTRIDE + PHIST + N_META + SEQ
PP = SEQS * PSTRIDE
CKEEP = HIST * (SEQS + 1)
PKEEP = PHIST * (SEQS + 1)

UT = 8
RING = 4
OUT_UNITS = 3
AHEAD = 2

G_F1A, G_F1B, G_MA, G_MB, G_F2A, G_F2B = (KD * i for i in range(6))
G_SSD = 6 * KD
G_D = G_SSD + KI
G_PS = G_D + KI
G_CB = G_PS + KD
G_CW = G_CB + NXBC
G_DTB = G_CW + CONV_K * NXBC
G_AL = G_DTB + N_HEADS
NPAR = G_AL + N_HEADS

C_ID = 0
C_TRI1 = C_ID + P
C_TRI0 = C_TRI1 + P
C_LAT1 = C_TRI0 + P
C_LAT0 = C_LAT1 + P
C_ONE = C_LAT0 + P
C_META = C_ONE + P
C_SEL = C_META + P
C_BLK = C_SEL + N_HEADS
C_CNT = C_BLK + SEQS
NCON = C_CNT + 4 * PHIST

N_G = 2 * (2 * KF + KD) + 2 * N_GROUPS + 2 * KI + 2 * KD + KD + KD + 2 * KD + KD
N_A = 3 * KD
N_B = 2 * KF + KI + 3 * KD
N_HI = N_A + N_B
N_VAL = 2 * KF + KI + 2 * KD + 3 * KD
N_GATE = 2 * KF + KI + 2 * KD
N_SQ = 3 * KD + 3 * KD + KI
N_SUM = 3 * KD
N_STAT = 7
N_PBT = 3

ST_F1A, ST_F1B, ST_MA, ST_Y, ST_MB, ST_F2A, ST_F2B = range(N_STAT)

V_F1, V_X1, V_Y = 0, KF, KF + KD
V_U = V_Y + KI
V_MG, V_X2, V_F2 = V_U + KD, V_U + 2 * KD, V_U + 3 * KD
H_F1, H_X1, H_Y = KD, KD + KF, 2 * KD + KF
H_U = H_Y + KI
H_PW, H_MG, H_X2, H_F2 = (H_U + KD * i for i in range(1, 5))
S_F1, S_X1, S_Y = KD, 2 * KD, 3 * KD
S_WO, S_X2, S_F2 = (S_Y + KI + KD * i for i in range(3))
MASKED = -30000.0

PHASES = {
    "f1i": (2 * KF, 2 * KF), "f1o": (OUT_UNITS * KD, KD), "bc": (2 * N_GROUPS, 2 * N_GROUPS),
    "ssd": (2 * KI, 2 * KI), "sbr": (3 * KD, 2 * KD), "u": (KD, KD), "pw": (N_GROUPS, KD),
    "pbr": (2 * KD, 2 * KD), "wo": (KD, KD), "f2i": (2 * KF, 2 * KF), "f2o": (OUT_UNITS * KD, KD),
}
U0, M0 = {}, {}
UNITS = N_M = 0
for _name, (_u, _m) in PHASES.items():
    U0[_name], M0[_name] = UNITS, N_M
    UNITS, N_M = UNITS + _u, N_M + _m
assert N_M == N_G and UNITS % RING == 0 and all(v % RING == 0 for v in (*U0.values(), *M0.values()))

assert U0["ssd"] % RING == 0
def z_at(t, last):
    return 2 * t + (1 if last else 2)


SO = SEQS * P + P
DK = 3 * N_HEADS


def rep(ap, n, at):
    v = ap.unsqueeze(at)
    shape = list(v.shape)
    shape[at] = n
    return v.broadcast_to(shape)


def seqs(ap, stride):
    return ap.rearrange("p (b s) -> p b s", s=stride)


def build(nc, x_in, wts, par_in, con_in, own_dram, dtw_in, cst_in, pst_in, ssm_in, y_out, ssm_out, conv_out, pool_out):
    with ExitStack() as ctx:
        def sb(name, shape, dt=F32):
            return ctx.enter_context(nc.sbuf_tensor(name, shape, dt))

        def sem(name):
            return ctx.enter_context(nc.semaphore(name))

        align = 32
        b_at = -(-nc.sbuf_base // align) * align
        bhi = sb("bhi", [P, KF, T], F32R)
        blo = sb("blo", [P, KF, T], F32R)
        tail_at = [b_at + KI * T * 4, b_at + (KF + KI) * T * 4]
        tail = [nc.alloc_sbuf_tensor_at(f"tail{i}", [P, (KF - KI) * T], F32, offset=o) for i, o in enumerate(tail_at)]
        x = sb("x", [P, KD, T])
        ahi = sb("ahi", [P, KD, T], F32R)
        alo = sb("alo", [P, KD, T], F32R)
        wraw = sb("wraw", [P, RING, UT * P])
        whi = sb("whi", [P, RING, UT * P], F32R)
        wlo = sb("wlo", [P, RING, UT * P], F32R)
        fo = sb("fo", [P, KD, T])
        bc = sb("bc", [P, 2 * N_GROUPS, T])
        par = sb("par", [P, DEPTH, NPAR])
        con = sb("con", [P, NCON])
        maskr = sb("maskr", [P, 2 * P], F32R)
        identr = sb("identr", [P, P], F32R)
        halfr = sb("halfr", [HEAD_DIM, 2 * P], F32R)
        eps = sb("eps", [P, 2])
        acc = sb("acc", [P, T])
        rpre = sb("rpre", [P, T])
        rpost = sb("rpost", [P, T])
        t_a = sb("t_a", [P, RING, T])
        t_b = sb("t_b", [P, RING, T])
        sq = sb("sq", [P, RING, T])
        xp = sb("xp", [P, CW])
        cv = sb("cv", [P, CW - HIST])
        cst = sb("cst", [P, NXBC, SEQS * HIST])
        cso = sb("cso", [P, CKEEP])
        dtw = sb("dtw", [P, KD, N_HEADS])
        dthi = sb("dthi", [P, KD, N_HEADS], F32R)
        dtlo = sb("dtlo", [P, KD, N_HEADS], F32R)
        rtok = sb("rtok", [P, 2, 3])
        ea = sb("ea", [P, N_HEADS])
        ss = sb("ss", [P, T], F32R)
        lst = sb("lst", [P, T], F32R)
        dec = sb("dec", [P, 2 * DK + SEQS * N_HEADS])
        rx = sb("rx", [P, 2, T], F32R)
        ztile = sb("ztile", [P, P])
        st = sb("st", [P, SEQS * P])

        class Carve:
            def __init__(self, ap):
                self.ap, self.at = ap, 0

            def take(self, *shape, rows=P):
                n = 1
                for d in shape:
                    n *= d
                v = self.ap[0:rows, self.at:self.at + n]
                self.at += n
                if len(shape) > 1:
                    names = "abc"[:len(shape)]
                    v = v.rearrange(f"p ({' '.join(names)}) -> p {' '.join(names)}", **dict(zip(names, shape)))
                return v

        def flat(t):
            return t[:, :, :].rearrange("p a b -> p (a b)")

        c = Carve(flat(fo))
        cb = c.take(N_GROUPS, T)
        pst = c.take(2, P)
        bm = c.take(SEQS, P, rows=SAMPLE)
        c = Carve(flat(sq))
        sp = c.take(6, DK)
        a4 = c.take(3, 4, N_HEADS)
        c = Carve(flat(sq)[:, T:])
        lx = c.take(4 * P)
        lx0 = c.take(2, CHUNKS[0][1])
        eab = c.take(T)
        xs = t_b[:, 2:4, :]
        c = Carve(tail[0][:, :])
        bt = c.take(N_GROUPS, 3, P)
        bcur = c.take(3, P)
        ph = Carve(tail[0][:, :]).take(KD, SEQS * PHIST)
        c = Carve(tail[1][:, :])
        so = c.take(SO)
        xdt = c.take(3, P)
        xdec = c.take(3, P)
        dt = c.take(3, N_HEADS)
        pso = Carve(tail[1][:, :]).take(KD, PKEEP)
        up = [flat(t_b)[:, 2 * i * T:2 * i * T + PW] for i in range(2)]
        win = [flat(t_a)[:, 2 * i * T:2 * i * T + PW] for i in range(2)]
        own_in = flat(t_a)[:, 0:4 * P]

        gb = [ctx.enter_context(nc.psum_tensor(f"gb{i}", [P, 512], F32)) for i in range(RING)]
        kb = [ctx.enter_context(nc.psum_tensor(f"kb{i}", [P, 512], F32)) for i in range(4)]

        s_in = sem("inputs_landed")
        s_eps = sem("eps_ready")
        s_hist = sem("histories_landed")
        s_hfree = sem("histories_used")
        w_landed = [sem(f"w_landed{i}") for i in range(RING)]
        w_rawfree = sem("w_raw_free")
        w_hi = sem("w_hi_ready")
        w_lo = sem("w_lo_ready")
        w_free = sem("w_free")
        g_full = sem("gemm_bank_full")
        g_out = sem("gemm_bank_evicted")
        a_done = sem("a_tile_ready")
        b_done = sem("b_tile_ready")
        hi_done = sem("hi_part_ready")
        gate_done = sem("gate_ready")
        val_in = sem("value_ready")
        sum_done = sem("square_of_output_summed")
        sq_done = sem("square_ready")
        stat_full = sem("mean_square_ready")
        sd_done = sem("rms_ready")
        consts = sem("constants_ready")
        cv_in = sem("conv_sum_ready")
        xbc_done = sem("xbc_tile_ready")
        dtw_hi = sem("dt_weights_hi")
        dtw_lo = sem("dt_weights_lo")
        dt_full = sem("dt_product_ready")
        dt_a = sem("dt_step_for_act")
        dt_b = sem("dt_step_by_act")
        a4_done = sem("log_decays_ready")
        cum_full = sem("cumulated_ready")
        dec_done = sem("decays_ready")
        ss_done = sem("cumulated_split")
        cbt_full = sem("cb_or_bt_full")
        cbt_free = sem("cb_or_bt_evicted")
        rx_done = sem("head_rows_ready")
        l_full = sem("log_l_ready")
        l_exp = sem("l_ready")
        e_exp = sem("decay_per_channel_ready")
        st_dec = sem("states_decayed")
        xt_full = sem("x_transposed")
        xd_done = sem("xdt_ready")
        m_done = sem("masked_cb_ready")
        cs_full = sem("chunk_states_ready")
        p_done = sem("states_chained")
        y_full = sem("y_products_ready")
        su_full = sem("sample_update_ready")
        so_done = sem("new_states_ready")
        so_free = sem("new_states_stored")
        st_landed = sem("states_landed")
        s_ph = sem("pool_history_landed")
        cso_done = sem("conv_rows_staged")
        cso_free = sem("conv_rows_stored")
        pso_done = sem("pool_rows_staged")
        pso_free = sem("pool_rows_stored")
        s_out = sem("y_stored")

        def cc(c, n=P, rows=P):
            return con[0:rows, c:c + n]

        def tri(c):
            return (C_TRI0 if c == 0 else C_TRI1)

        block = ctx.enter_context(nc.Block())

        @block.sync
        def _(sp_):
            sp_.dma_start(x[:, :, :], x_in).then_inc(s_in, 16)
            sp_.dma_start(par[:, :, :], par_in).then_inc(s_in, 16)
            sp_.dma_start(con[:, :], con_in).then_inc(s_in, 16)
            sp_.dma_start(own_in, own_dram).then_inc(s_in, 16)

            def unit(u, slot):
                sp_.wait_ge(w_rawfree, u + 1)
                sp_.dma_start(wraw[:, slot, :], wts[u, :, :]).then_inc(w_landed[slot], 16)

            with sp_.Fori(0, DEPTH) as L:
                sp_.wait_ge(s_hfree, L + 1)
                sp_.dma_start(dtw[:, :, :], dtw_in[L, :, :, :]).then_inc(s_hist, 16)
                sp_.dma_start(cst[:, :, :], cst_in[L, :, :, :]).then_inc(s_hist, 16)
                with sp_.Fori(0, UNITS // RING) as i:
                    for s in range(RING):
                        unit(L * UNITS + RING * i + s, s)
            for s in range(AHEAD):
                sp_.wait_ge(w_rawfree, DEPTH * UNITS + s + 1)
                sp_.dma_start(wraw[:, s, :], wts[s, :, :]).then_inc(w_landed[s], 16)

        @block.gpsimd
        def _(pool):
            pool.sem_inc(w_rawfree, RING)

            def lo(u, s):
                pool.wait_ge(w_hi, u + 1)
                pool.tensor_tensor(wlo[:, s, :], wraw[:, s, :], whi[:, s, :].bitcast(F32), ALU.subtract).then_inc(w_lo, 1)
                pool.wait_ge(w_lo, u + 1)
                pool.sem_inc(w_rawfree, 1)

            def ahead(L, u, slot):
                lo(L * UNITS + u + AHEAD, (slot + AHEAD) % RING)

            def some(L, u0, u1):
                with pool.Fori(0, (u1 - u0) // RING) as i:
                    for s in range(RING):
                        ahead(L, u0 + RING * i + s, s)

            def ssd_step(L, t, q, last):
                u = U0["ssd"] + 2 * t
                if not last:
                    ahead(L, u + 1, 2 * q + 1)
                pool.wait_ge(dec_done, L + 1)
                pool.wait_ge(st_landed, 16 * (L * KI + t) + 16)
                pool.wait_ge(so_free, 16 * (L * KI + t) + 16)
                ds_ = dec[:, 2 * DK:].rearrange("p (b h) -> p b h", b=SEQS)[:, :, bass.ds(2 * t, 2)]
                pool.tensor_tensor(so[:, 0:SEQS * P].rearrange("p (b h d) -> p b h d", b=SEQS, h=2),
                                   st[:, :].rearrange("p (b h d) -> p b h d", b=SEQS, h=2), rep(ds_, HEAD_DIM, 3), ALU.mult).then_inc(st_dec, 1)
                ahead(L, U0["ssd"] + z_at(t, last), 3 if last else (2 * q + 2) % RING)

            for s in range(AHEAD):
                lo(s, s)
            with pool.Fori(0, DEPTH) as L:
                some(L, 0, U0["ssd"])
                ahead(L, U0["ssd"], 0)
                with pool.Fori(0, KI // 2 - 1) as i:
                    for q in range(2):
                        ssd_step(L, 2 * i + q, q, False)
                for q in range(2):
                    ssd_step(L, KI - 2 + q, q, q == 1)
                some(L, U0["sbr"], UNITS)

        @block.scalar
        def _(act):
            act.sem_inc(xbc_done, 1)
            act.wait_ge(s_in, 64)
            act.activation(maskr[:, :], own_in[:, 0:2 * P], ACT.Copy)
            act.activation(identr[:, :], cc(C_ID), ACT.Copy)
            act.activation(halfr[:, :], own_in[0:HEAD_DIM, 2 * P:4 * P], ACT.Copy).then_inc(consts, 1)

            def split(L, u, slot):
                act.wait_ge(w_landed[slot], L * (UNITS // RING * 16) + (u - slot) * (16 // RING) + 16)
                act.wait_ge(w_free, L * UNITS + u + 1)
                act.activation(whi[:, slot, :], wraw[:, slot, :], ACT.Copy).then_inc(w_hi, 1)

            def ahead(L, u, slot):
                split(L, u + AHEAD, (slot + AHEAD) % RING)

            def root(L, n):
                act.wait_ge(stat_full, L * N_STAT + n + 1)
                e = 1 if n in (ST_F1B, ST_F2B) else 0
                scale = (4.0 if e else 1.0) / (D_INNER if n == ST_Y else D_MODEL)
                act.activation(kb[0][:, 0:T], kb[0][:, 0:T], ACT.Sqrt, bias=eps[:, e:e + 1], scale=scale).then_inc(sd_done, 1)

            def split_x(L, gain, a0, v0):
                for k in range(KD):
                    if v0 is None:
                        act.wait_ge(val_in, L * N_VAL + 1)
                    else:
                        act.wait_ge(val_in, L * N_VAL + v0 + k + 2)
                    if k >= RING:
                        act.wait_ge(a_done, L * N_A + a0 + k - RING + 1)
                    act.activation(ahi[:, k, :], x[:, k, :], ACT.Copy, scale=par[:, L, gain + k:gain + k + 1]).then_inc(hi_done, 1)
                    act.activation(sq[:, k % RING, :], x[:, k, :], ACT.Square).then_inc(sq_done, 1)

            def ffn_in(L, ph_, v0):
                u0, m0 = U0[ph_], M0[ph_]
                with act.Fori(0, KF // 2) as i:
                    for q in range(2):
                        ahead(L, u0 + RING * i + 2 * q, 2 * q)
                        act.wait_ge(g_out, L * N_G + m0 + RING * i + 2 * q + 1 + RING)
                        act.activation(t_b[:, 2 * q, :], t_a[:, 2 * q, :], ACT.Silu).then_inc(gate_done, 1)
                        ahead(L, u0 + RING * i + 2 * q + 1, 2 * q + 1)
                        act.wait_ge(val_in, L * N_VAL + v0 + 2 * i + q + 2)
                        act.activation(bhi[:, 2 * i + q, :], t_b[:, 2 * q + 1, :], ACT.Copy).then_inc(hi_done, 1)

            def out_squares(L, ph_, units):
                with act.Fori(0, KD // RING) as i:
                    for j in range(RING):
                        for s in range(units):
                            ahead(L, U0[ph_] + RING * units * i + units * j + s, (units * j + s) % RING)
                        act.wait_ge(g_out, L * N_G + M0[ph_] + RING * i + j + 1 + RING)
                        act.activation(sq[:, j, :], fo[:, RING * i + j, :], ACT.Square).then_inc(sq_done, 1)

            def silu_xbc(L, c, dst):
                act.wait_ge(cv_in, L * NXBC + c + 1)
                bias = par[:, L, bass.ds(G_CB + c, 1)]
                act.activation(seqs(dst[:, 0:SAMPLE], STEPS), seqs(cv[:, 0:CP], CSTRIDE)[:, :, 0:STEPS], ACT.Silu, bias=bias)
                act.activation(dst[:, SAMPLE:T], cv[:, CP:CW - HIST], ACT.Silu, bias=bias).then_inc(xbc_done, 1)

            def store_conv_rows(L, c):
                act.wait_ge(cso_done, L * NXBC + c + 1)
                act.dma_start(conv_out[L * NXBC + c, :, :], cso[:, :]).then_inc(cso_free, 16)

            def head_rows(L, t):
                for h in range(2):
                    ins = act.activation(rx[:, h, :], ss[:, :].bitcast(F32), ACT.Copy, scale=con[:, bass.ds(C_SEL + 2 * t + h, 1)])
                ins.then_inc(rx_done, 1)

            def exp_l(L, t):
                act.wait_ge(l_full, L * KI + t + 1)
                act.activation(lx, gb[2][:, :], ACT.Exp)
                n0 = CHUNKS[0][1]
                act.activation(lx0[0:n0, :, :].rearrange("p a b -> p (a b)"), gb[3][0:n0, 0:2 * n0], ACT.Exp).then_inc(l_exp, 1)

            def exp_e():
                act.activation(eab[:, :], gb[3][:, 2 * CHUNKS[0][1]:2 * CHUNKS[0][1] + T], ACT.Exp).then_inc(e_exp, 1)

            def ssd_step(L, t, q, last):
                u = U0["ssd"] + 2 * t
                if not last:
                    head_rows(L, t + 1)
                    ahead(L, u + 1, 2 * q + 1)
                    silu_xbc(L, 2 * N_GROUPS + t + 1, xs[:, 1 - q, :])
                    store_conv_rows(L, 2 * N_GROUPS + t + 1)
                z = z_at(t, last)
                ahead(L, U0["ssd"] + z, 3 if last else (2 * q + 2) % RING)
                act.wait_ge(g_out, L * N_G + M0["ssd"] + z + 1 + RING)
                act.activation(t_b[:, 0, :], t_b[:, 1, :], ACT.Silu).then_inc(gate_done, 1)
                if not last:
                    exp_l(L, t + 1)
                act.wait_ge(val_in, L * N_VAL + V_Y + t + 2)
                if not last:
                    exp_e()
                    act.wait_ge(st_dec, L * KI + t + 1)
                    load_states(L, t + 1)
                act.activation(bhi[:, t, :], t_a[:, 3, :], ACT.Copy, scale=par[:, L, bass.ds(G_SSD + t, 1)]).then_inc(hi_done, 1)
                act.activation(sq[:, 0, :], t_a[:, 3, :], ACT.Square).then_inc(sq_done, 1)
                act.wait_ge(so_done, L * KI + t + 1)
                act.dma_start(ssm_out[L * KI + t, :, :], so).then_inc(so_free, 16)

            def load_states(L, t):
                act.dma_start(st[:, :], ssm_in[L * KI + t, :, :]).then_inc(st_landed, 16)

            for s in range(AHEAD):
                split(0, s, s)
            act.wait_ge(s_eps, 1)
            with act.Fori(0, DEPTH) as L:
                act.wait_ge(s_hist, (L + 1) * 32)
                act.activation(dthi[:, :, :], dtw[:, :, :], ACT.Copy).then_inc(dtw_hi, 1)
                split_x(L, G_F1A, 0, None)
                root(L, ST_F1A)
                ffn_in(L, "f1i", V_F1)
                out_squares(L, "f1o", OUT_UNITS)
                root(L, ST_F1B)
                split_x(L, G_MA, KD, V_X1)
                root(L, ST_MA)
                act.wait_ge(dt_full, L + 1)
                act.activation(rtok[:, 0, :], kb[1][:, DK:DK + 3], ACT.Sqrt, bias=eps[:, 0:1], scale=1.0 / D_MODEL).then_inc(dt_b, 1)
                act.wait_ge(dt_a, L * 2 + 1)
                act.activation(ea[:, :], par[:, L, G_AL:G_AL + N_HEADS], ACT.Exp)
                act.activation(sp[:, 2, :], sp[:, 1, :], ACT.Exp, scale=-1.0).then_inc(dt_b, 1)
                act.wait_ge(dt_a, L * 2 + 2)
                act.activation(sp[:, 4, :], sp[:, 3, :], ACT.Ln).then_inc(dt_b, 1)
                with act.Fori(0, 2 * N_GROUPS // RING) as i:
                    for j in range(RING):
                        ahead(L, U0["bc"] + RING * i + j, j)
                        silu_xbc(L, RING * i + j, bc[:, RING * i + j, :])
                        store_conv_rows(L, RING * i + j)
                act.wait_ge(cum_full, L + 1)
                act.activation(dec[:, :], kb[3][:, 0:2 * DK + SEQS * N_HEADS], ACT.Exp).then_inc(dec_done, 1)
                ahead(L, U0["ssd"], 0)
                silu_xbc(L, 2 * N_GROUPS, xs[:, 0, :])
                store_conv_rows(L, 2 * N_GROUPS)
                act.wait_ge(ss_done, L + 1)
                load_states(L, 0)
                head_rows(L, 0)
                exp_l(L, 0)
                exp_e()
                with act.Fori(0, KI // 2 - 1) as i:
                    for q in range(2):
                        ssd_step(L, 2 * i + q, q, False)
                for q in range(2):
                    ssd_step(L, KI - 2 + q, q, q == 1)
                act.dma_start(ph, pst_in[L, :, :, :]).then_inc(s_ph, 16)
                root(L, ST_Y)
                with act.Fori(0, KD // RING) as i:
                    for j in range(RING):
                        for s in range(3):
                            ahead(L, U0["sbr"] + 3 * RING * i + 3 * j + s, (3 * j + s) % RING)
                            if s == 0:
                                act.wait_ge(g_out, L * N_G + M0["sbr"] + 2 * RING * i + 2 * j + 1 + RING)
                                act.activation(t_b[:, 2 * (j % 2), :], t_a[:, 2 * (j % 2), :], ACT.Sigmoid).then_inc(gate_done, 1)
                for k in range(KD):
                    ahead(L, U0["u"] + k, k % RING)
                    act.wait_ge(val_in, L * N_VAL + V_U + k + 2)
                    act.activation(bhi[:, k, :], sq[:, k % RING, :], ACT.Copy).then_inc(hi_done, 1)
                act.wait_ge(pso_done, L + 1)
                act.dma_start(pool_out[L, :, :, :], pso).then_inc(pso_free, 16)
                for g in range(N_GROUPS):
                    ahead(L, U0["pw"] + g, g)
                    for mm in range(2):
                        m = 2 * g + mm
                        act.wait_ge(g_full, L * N_G + M0["pw"] + m + 1)
                        act.activation(bhi[:, KD + m, :], gb[m % RING][:, 0:T], ACT.Copy,
                                       scale=par[:, L, G_PS + m:G_PS + m + 1]).then_inc(hi_done, 1)
                with act.Fori(0, KD // 2) as i:
                    for j in range(2):
                        ahead(L, U0["pbr"] + RING * i + 2 * j, 2 * j)
                        act.wait_ge(g_out, L * N_G + M0["pbr"] + RING * i + 2 * j + 1 + RING)
                        act.activation(t_b[:, 2 * j, :], t_a[:, 2 * j, :], ACT.Sigmoid).then_inc(gate_done, 1)
                        ahead(L, U0["pbr"] + RING * i + 2 * j + 1, 2 * j + 1)
                        act.wait_ge(val_in, L * N_VAL + V_MG + 2 * i + j + 2)
                        act.activation(bhi[:, 2 * i + j, :], t_b[:, 2 * j + 1, :], ACT.Copy).then_inc(hi_done, 1)
                out_squares(L, "wo", 1)
                root(L, ST_MB)
                split_x(L, G_F2A, 2 * KD, V_X2)
                root(L, ST_F2A)
                ffn_in(L, "f2i", V_F2)
                out_squares(L, "f2o", OUT_UNITS)
                root(L, ST_F2B)
            act.wait_ge(val_in, DEPTH * N_VAL + 1)
            act.dma_start(y_out, x[:, :, :]).then_inc(s_out, 16)
            act.wait_ge(s_out, 16)
            act.wait_ge(cso_free, 16 * (DEPTH * NXBC + 1))
            act.wait_ge(pso_free, 16 * DEPTH)
            act.wait_ge(so_free, 16 * (DEPTH * KI + 1))

        @block.vector
        def _(dve):
            dve.sem_inc(g_out, RING)
            dve.sem_inc(s_hfree, 1)
            dve.sem_inc(cso_free, 16)
            dve.sem_inc(so_free, 16)
            dve.memset(eps[:, 0:1], EPS)
            dve.memset(eps[:, 1:2], 4 * EPS).then_inc(s_eps, 1)
            dve.memset(ztile[:, :], 0.0)
            dve.memset(xp[:, :], 0.0)
            dve.memset(ss[:, :].bitcast(F32), 1.0)
            dve.memset(lst[:, :].bitcast(F32), 1.0).then_inc(consts, 1)
            dve.wait_ge(s_in, 64)
            dve.sem_inc(val_in, 1)

            def pcol(L, c):
                return par[:, L, bass.ds(c, 1)]

            def inverse(L, n, dst):
                dve.wait_ge(sd_done, L * N_STAT + n + 1)
                dve.reciprocal(dst[:, :], kb[0][:, 0:T])
                dve.drain()

            def clear_acc():
                dve.memset(acc[:, :], 0.0)
                dve.drain()

            def split_tile(L, k, gain, a0, h0, s0):
                dve.wait_ge(sq_done, L * N_SQ + s0 + k + 1)
                dve.tensor_tensor(acc[:, :], acc[:, :], sq[:, k % RING, :], ALU.add)
                dve.wait_ge(hi_done, L * N_HI + h0 + k + 1)
                dve.scalar_tensor_tensor(alo[:, k, :], x[:, k, :], pcol(L, gain + k), ahi[:, k, :].bitcast(F32),
                                         ALU.mult, ALU.subtract).then_inc(a_done, 1)

            def update_x(L, gain, nxt=None):
                lag = 3
                for s in range(KD + 1 + (lag if nxt else 0)):
                    if s < KD:
                        dve.scalar_tensor_tensor(t_a[:, s % RING, :], fo[:, s, :], pcol(L, gain + s), rpost[:, :], ALU.mult, ALU.mult)
                    if 1 <= s <= KD:
                        dve.tensor_tensor(x[:, s - 1, :], x[:, s - 1, :], t_a[:, (s - 1) % RING, :], ALU.add).then_inc(val_in, 1)
                    if nxt and s > lag:
                        split_tile(L, s - lag - 1, *nxt)
                    dve.drain()

            def ffn_in(L, ph_, h0, gt0):
                m0 = M0[ph_]
                with dve.Fori(0, KF // 2) as i:
                    for q in range(2):
                        for part in range(2):
                            r = 2 * q + part
                            dve.wait_ge(g_full, L * N_G + m0 + RING * i + r + 1)
                            dve.tensor_tensor(t_a[:, r, :], gb[r][:, 0:T], rpre[:, :], ALU.mult).then_inc(g_out, 1)
                        dve.drain()
                        dve.wait_ge(gate_done, L * N_GATE + gt0 + 2 * i + q + 1)
                        dve.tensor_tensor(t_b[:, 2 * q + 1, :], t_a[:, 2 * q + 1, :], t_b[:, 2 * q, :], ALU.mult).then_inc(val_in, 1)
                        dve.wait_ge(hi_done, L * N_HI + h0 + 2 * i + q + 1)
                        dve.tensor_tensor(blo[:, 2 * i + q, :], t_b[:, 2 * q + 1, :], bhi[:, 2 * i + q, :].bitcast(F32),
                                          ALU.subtract).then_inc(b_done, 1)

            def out_tiles(L, ph_, s0):
                clear_acc()
                with dve.Fori(0, KD // RING) as i:
                    for j in range(RING):
                        dve.wait_ge(g_full, L * N_G + M0[ph_] + RING * i + j + 1)
                        dve.tensor_copy(fo[:, RING * i + j, :], gb[j][:, 0:T]).then_inc(g_out, 1)
                        dve.wait_ge(sq_done, L * N_SQ + s0 + RING * i + j + 1)
                        dve.tensor_tensor(acc[:, :], acc[:, :], sq[:, j, :], ALU.add).then_inc(sum_done, 1)
                        dve.drain()

            def conv(L, c, m, bank):
                dve.wait_ge(g_full, L * N_G + m + 1)
                dve.wait_ge(cso_free, 16 * (L * NXBC + c + 1))
                h3 = seqs(xp[:, 0:CP], CSTRIDE)
                dve.tensor_copy(h3[:, :, 0:HIST], seqs(cst[:, c, :], HIST))
                dve.tensor_tensor(h3[:, :, HIST:CSTRIDE], seqs(gb[bank][:, 0:SAMPLE], STEPS), seqs(rpre[:, 0:SAMPLE], STEPS), ALU.mult)
                dve.tensor_tensor(xp[:, CP + HIST:CW], gb[bank][:, SAMPLE:T], rpre[:, SAMPLE:T], ALU.mult).then_inc(g_out, 1)
                dve.drain()
                dve.tensor_copy(seqs(cso[:, 0:SEQS * HIST], HIST), h3[:, :, STEPS:CSTRIDE])
                dve.tensor_copy(cso[:, SEQS * HIST:CKEEP], xp[:, CW - HIST:CW]).then_inc(cso_done, 1)
                n = CW - HIST
                dve.wait_ge(xbc_done, L * NXBC + c + 1)
                dve.tensor_scalar(cv[:, :], xp[:, 0:n], pcol(L, G_CW + CONV_K * c), None, ALU.mult)
                for k in range(1, CONV_K):
                    dve.drain()
                    ins = dve.scalar_tensor_tensor(cv[:, :], xp[:, k:k + n], pcol(L, G_CW + CONV_K * c + k), cv[:, :], ALU.mult, ALU.add)
                ins.then_inc(cv_in, 1)

            def group(g):
                dve.tensor_copy(bcur[:, :, :], bt[:, g, :, :])
                dve.tensor_tensor(bm[:, :, :], rep(bt[0:SAMPLE, g, 0, :], SEQS, 1), rep(con[0:SAMPLE, C_BLK:C_BLK + SEQS], P, 2), ALU.mult)

            def heads(ap, at=2):
                return rep(ap, HEAD_DIM, 3)

            def ssd_step(L, t, q, g, last):
                kt = L * KI + t
                dve.wait_ge(l_exp, kt + 1)
                n0 = CHUNKS[0][1]
                l4 = lx[:, :].rearrange("p (c h i) -> p c h i", c=2, h=2)
                dve.tensor_tensor(l4, l4, rep(cb[:, g, n0:T].rearrange("p (c i) -> p c i", c=2), 2, 2), ALU.mult)
                dve.tensor_tensor(lx0[0:n0, :, :], lx0[0:n0, :, :], rep(cb[0:n0, g, 0:n0], 2, 1), ALU.mult).then_inc(m_done, 1)
                dve.wait_ge(xt_full, kt + 1)
                xt = kb[0][:, 0:3 * P].rearrange("p (c h d) -> p c h d", c=3, h=2)
                v = [b[:, :, :].rearrange("p c (h d) -> p c h d", h=2) for b in (xdt, xdec)]
                dve.tensor_tensor(v[0], xt, heads(dt[:, :, bass.ds(2 * t, 2)]), ALU.mult)
                dve.drain()
                de = dec[:, 0:DK].rearrange("p (c h) -> p c h", c=3)[:, :, bass.ds(2 * t, 2)]
                dve.tensor_tensor(v[1], v[0], heads(de), ALU.mult).then_inc(xd_done, 1)
                if not last:
                    conv(L, 2 * N_GROUPS + t + 1, M0["ssd"] + 2 * t + 1, 0)
                dve.wait_ge(cs_full, kt + 1)
                dve.wait_ge(so_free, 16 * kt + 16)
                dve.tensor_copy(pst[:, 0, :], kb[3][:, 0:P])
                dve.drain()
                for c, dst in ((1, pst[:, 1, :]), (2, so[:, SEQS * P:SO])):
                    for h in range(2):
                        cols = slice(h * HEAD_DIM, (h + 1) * HEAD_DIM)
                        ins = dve.scalar_tensor_tensor(dst[:, cols], pst[:, c - 1, cols], dec[:, bass.ds(DK + c * N_HEADS + 2 * t + h, 1)],
                                                       kb[3][:, c * P + h * HEAD_DIM:c * P + (h + 1) * HEAD_DIM], ALU.mult, ALU.add)
                    if c == 1:
                        dve.drain()
                ins.then_inc(p_done, 1)
                z = M0["ssd"] + z_at(t, last)
                dve.wait_ge(g_full, L * N_G + z + 1)
                dve.tensor_tensor(t_b[:, 1, :], gb[1][:, 0:T], rpre[:, :], ALU.mult).then_inc(g_out, 1)
                dve.wait_ge(e_exp, kt + 1)
                dve.wait_ge(y_full, kt + 1)
                dve.tensor_tensor(t_a[:, 0, :], kb[1][:, 0:T], eab[:, :], ALU.mult)
                dve.drain()
                dve.tensor_tensor(t_a[:, 1, :], kb[0][:, 0:T], t_a[:, 0, :], ALU.add)
                dve.drain()
                dve.scalar_tensor_tensor(t_a[:, 2, :], xs[:, q, :], pcol(L, G_D + t), t_a[:, 1, :], ALU.mult, ALU.add)
                dve.drain()
                dve.wait_ge(gate_done, L * N_GATE + KF + t + 1)
                dve.tensor_tensor(t_a[:, 3, :], t_a[:, 2, :], t_b[:, 0, :], ALU.mult).then_inc(val_in, 1)
                dve.wait_ge(st_dec, kt + 1)
                dve.wait_ge(su_full, kt + 1)
                for b in range(2):
                    cols = slice(b * 4 * P, (b + 1) * 4 * P)
                    ins = dve.tensor_tensor(so[:, cols], so[:, cols], kb[2 + b][:, :], ALU.add)
                ins.then_inc(so_done, 1)
                dve.wait_ge(hi_done, L * N_HI + H_Y + t + 1)
                dve.wait_ge(sq_done, L * N_SQ + S_Y + t + 1)
                dve.tensor_tensor(acc[:, :], acc[:, :], sq[:, 0, :], ALU.add)
                dve.scalar_tensor_tensor(blo[:, t, :], t_a[:, 3, :], pcol(L, G_SSD + t), bhi[:, t, :].bitcast(F32),
                                         ALU.mult, ALU.subtract).then_inc(b_done, 1)
                dve.drain()

            with dve.Fori(0, DEPTH) as L:
                clear_acc()
                for k in range(KD):
                    split_tile(L, k, G_F1A, 0, 0, 0)
                    dve.drain()
                dve.wait_ge(dtw_hi, L + 1)
                dve.tensor_tensor(dtlo[:, :, :], dtw[:, :, :], dthi[:, :, :].bitcast(F32), ALU.subtract).then_inc(dtw_lo, 1)
                inverse(L, ST_F1A, rpre)
                ffn_in(L, "f1i", H_F1, 0)
                out_tiles(L, "f1o", S_F1)
                inverse(L, ST_F1B, rpost)
                clear_acc()
                update_x(L, G_F1B, (G_MA, KD, H_X1, S_X1))
                inverse(L, ST_MA, rpre)
                dve.wait_ge(dt_b, L * N_PBT + 1)
                dve.reciprocal(rtok[:, 1, :], rtok[:, 0, :])
                dve.drain()
                for c in range(3):
                    cols = slice(c * N_HEADS, (c + 1) * N_HEADS)
                    dve.scalar_tensor_tensor(sp[:, 0, cols], kb[1][:, cols], rtok[:, 1, c:c + 1], par[:, L, G_DTB:G_DTB + N_HEADS], ALU.mult, ALU.add)
                dve.drain()
                dve.scalar_tensor_tensor(sp[:, 1, :], sp[:, 0, :], -1.0, sp[:, 0, :], ALU.mult, ALU.max).then_inc(dt_a, 1)
                dve.wait_ge(dt_b, L * N_PBT + 2)
                dve.tensor_scalar(sp[:, 3, :], sp[:, 2, :], 1.0, None, ALU.add).then_inc(dt_a, 1)
                dve.drain()
                dve.tensor_scalar(sp[:, 5, :], sp[:, 3, :], -1.0, 1e-30, ALU.add, ALU.add)
                dve.drain()
                dve.reciprocal(sp[:, 1, :], sp[:, 5, :])
                dve.drain()
                dve.wait_ge(dt_b, L * N_PBT + 3)
                dve.tensor_scalar(sp[:, 5, :], sp[:, 4, :], 1e-30, None, ALU.add)
                dve.drain()
                dve.tensor_tensor(sp[:, 1, :], sp[:, 1, :], sp[:, 5, :], ALU.mult)
                dve.drain()
                dve.tensor_tensor(sp[:, 1, :], sp[:, 1, :], sp[:, 2, :], ALU.mult)
                dve.drain()
                dtf = dt[:, :, :].rearrange("p c h -> p (c h)")
                dve.scalar_tensor_tensor(dtf, sp[:, 0, :], 0.0, sp[:, 1, :], ALU.max, ALU.add)
                dve.drain()
                for c in range(3):
                    ins = dve.scalar_tensor_tensor(a4[:, c, :, :], rep(dt[:, c, :], 4, 1), -1.0, rep(ea[:, :], 4, 1), ALU.mult, ALU.mult)
                ins.then_inc(a4_done, 1)
                with dve.Fori(0, 2 * N_GROUPS // RING) as i:
                    for j in range(RING):
                        conv(L, RING * i + j, M0["bc"] + RING * i + j, j)
                dve.wait_ge(cum_full, L + 1)
                cum = kb[2]
                dve.tensor_copy(ss[0:64, :], cum[0:64, 0:T])
                dve.tensor_copy(lst[96:128, :], cum[96:128, 0:T])
                dve.tensor_scalar(lst[64:96, :], cum[64:96, 0:T], -1.0, None, ALU.mult)
                dve.drain()
                dve.tensor_tensor(ss[32:64, :], cum[32:64, 0:T], ss[32:64, :].bitcast(F32), ALU.subtract)
                dve.tensor_tensor(lst[96:128, :], lst[96:128, :].bitcast(F32), cum[96:128, 0:T], ALU.subtract).then_inc(ss_done, 1)
                for g in range(N_GROUPS):
                    dve.wait_ge(cbt_full, L * 2 * N_GROUPS + 2 * g + 1)
                    dve.tensor_copy(cb[:, g, :], kb[g][:, 0:T]).then_inc(cbt_free, 1)
                    dve.wait_ge(cbt_full, L * 2 * N_GROUPS + 2 * g + 2)
                    dve.tensor_copy(bt[:, g, :, :].rearrange("p c n -> p (c n)"), kb[g][:, 0:3 * P]).then_inc(cbt_free, 1)
                dve.wait_ge(dec_done, L + 1)
                conv(L, 2 * N_GROUPS, M0["ssd"], 0)
                clear_acc()
                with dve.Fori(0, KI // 2 - 1) as i:
                    group(i // 2)
                    dve.drain()
                    for q in range(2):
                        ssd_step(L, 2 * i + q, q, i // 2, False)
                group(N_GROUPS - 1)
                dve.drain()
                for q in range(2):
                    ssd_step(L, KI - 2 + q, q, N_GROUPS - 1, q == 1)
                inverse(L, ST_Y, rpost)
                with dve.Fori(0, KD // RING) as i:
                    for j in range(RING):
                        m, r = M0["sbr"] + 2 * RING * i + 2 * j, 2 * (j % 2)
                        dve.wait_ge(g_full, L * N_G + m + 1)
                        dve.tensor_tensor(t_a[:, r, :], gb[r][:, 0:T], rpre[:, :], ALU.mult).then_inc(g_out, 1)
                        dve.wait_ge(g_full, L * N_G + m + 2)
                        dve.tensor_tensor(t_a[:, r + 1, :], gb[r + 1][:, 0:T], rpost[:, :], ALU.mult).then_inc(g_out, 1)
                        dve.drain()
                        dve.wait_ge(gate_done, L * N_GATE + KF + KI + RING * i + j + 1)
                        dve.tensor_tensor(fo[:, RING * i + j, :], t_a[:, r + 1, :], t_b[:, r, :], ALU.mult)
                dve.drain()
                cnt = con[:, C_CNT:C_CNT + 4 * PHIST].rearrange("p (w c) -> p w c", w=4)
                for i in range(2):
                    dve.memset(up[i][:, PP:PP + PHIST], 0.0)
                dve.drain()
                dve.wait_ge(s_ph, 16 * (L + 1))
                dve.wait_ge(so_free, 16 * (L + 1) * KI + 16)
                for k in range(KD):
                    w = k // 2
                    b = up[k % 2]
                    dve.wait_ge(g_full, L * N_G + M0["u"] + k + 1)
                    h3 = seqs(b[:, 0:PP], PSTRIDE)
                    dve.tensor_copy(h3[:, :, 0:PHIST], seqs(ph[:, k, :], PHIST))
                    dve.tensor_tensor(h3[:, :, PHIST:PSTRIDE], seqs(gb[k % RING][:, 0:SAMPLE], STEPS), seqs(rpre[:, 0:SAMPLE], STEPS), ALU.mult)
                    dve.tensor_tensor(b[:, PP + PHIST:PW], gb[k % RING][:, SAMPLE:T], rpre[:, SAMPLE:T], ALU.mult).then_inc(g_out, 1)
                    dve.drain()
                    dve.tensor_copy(seqs(pso[:, k, 0:SEQS * PHIST], PHIST), h3[:, :, STEPS:PSTRIDE])
                    ins = dve.tensor_copy(pso[:, k, SEQS * PHIST:PKEEP], b[:, PW - PHIST:PW])
                    if k == KD - 1:
                        ins.then_inc(pso_done, 1)
                    src, done = b, 0
                    for lvl in range(w + 1):
                        step = 1 << lvl
                        dst = win[lvl % 2]
                        dve.tensor_tensor(dst[:, done + step:PW], src[:, done + step:PW], src[:, done:PW - step], ALU.add)
                        dve.drain()
                        src, done = dst, done + step
                    p0 = PP + PHIST
                    dve.tensor_tensor(src[:, p0:p0 + PHIST], src[:, p0:p0 + PHIST], cnt[:, w, :], ALU.mult)
                    dve.drain()
                    if k >= RING:
                        dve.wait_ge(hi_done, L * N_HI + H_U + k - RING + 1)
                    o = sq[:, k % RING, :]
                    inv = 1.0 / (1 << (w + 1))
                    dve.scalar_tensor_tensor(seqs(o[:, 0:SAMPLE], STEPS), seqs(src[:, 0:PP], PSTRIDE)[:, :, PHIST:PSTRIDE], inv,
                                             h3[:, :, PHIST:PSTRIDE], ALU.mult, ALU.subtract)
                    dve.scalar_tensor_tensor(o[:, SAMPLE:T], src[:, p0:PW], inv, b[:, p0:PW], ALU.mult, ALU.subtract).then_inc(val_in, 1)
                    dve.wait_ge(hi_done, L * N_HI + H_U + k + 1)
                    dve.tensor_tensor(blo[:, k, :], o, bhi[:, k, :].bitcast(F32), ALU.subtract).then_inc(b_done, 1)
                dve.sem_inc(s_hfree, 1)
                for m in range(KD):
                    dve.wait_ge(hi_done, L * N_HI + H_PW + m + 1)
                    dve.scalar_tensor_tensor(blo[:, KD + m, :], gb[m % RING][:, 0:T], par[:, L, G_PS + m:G_PS + m + 1],
                                             bhi[:, KD + m, :].bitcast(F32), ALU.mult, ALU.subtract).then_inc(b_done, 1)
                    dve.drain()
                    dve.sem_inc(g_out, 1)
                with dve.Fori(0, KD // 2) as i:
                    for j in range(2):
                        m, r = M0["pbr"] + RING * i + 2 * j, 2 * j
                        dve.wait_ge(g_full, L * N_G + m + 1)
                        dve.tensor_tensor(t_a[:, r, :], gb[r][:, 0:T], rpre[:, :], ALU.mult).then_inc(g_out, 1)
                        dve.wait_ge(gate_done, L * N_GATE + KF + KI + KD + 2 * i + j + 1)
                        dve.wait_ge(g_full, L * N_G + m + 2)
                        dve.tensor_tensor(t_a[:, r + 1, :], gb[r + 1][:, 0:T], t_b[:, r, :], ALU.mult).then_inc(g_out, 1)
                        dve.drain()
                        dve.tensor_tensor(t_b[:, r + 1, :], t_a[:, r + 1, :], fo[:, 2 * i + j, :], ALU.add).then_inc(val_in, 1)
                        dve.wait_ge(hi_done, L * N_HI + H_MG + 2 * i + j + 1)
                        dve.tensor_tensor(blo[:, 2 * i + j, :], t_b[:, r + 1, :], bhi[:, 2 * i + j, :].bitcast(F32),
                                          ALU.subtract).then_inc(b_done, 1)
                out_tiles(L, "wo", S_WO)
                inverse(L, ST_MB, rpost)
                clear_acc()
                update_x(L, G_MB, (G_F2A, 2 * KD, H_X2, S_X2))
                dve.wait_ge(pso_free, 16 * (L + 1))
                inverse(L, ST_F2A, rpre)
                ffn_in(L, "f2i", H_F2, KF + KI + 2 * KD)
                out_tiles(L, "f2o", S_F2)
                inverse(L, ST_F2B, rpost)
                update_x(L, G_F2B)

        @block.tensor
        def _(pe):
            pe.sem_inc(w_free, RING - 1)
            pe.wait_ge(consts, 2)

            def unit(L, u, slot, bank, hi, lo, k0, first, last, tiles=UT, w0=0, fresh=True):
                if fresh:
                    pe.wait_ge(w_lo, L * UNITS + u + 1)
                for j in range(tiles):
                    w = slice((w0 + j) * P, (w0 + j + 1) * P)
                    xh, xl = hi[:, k0 + j, :], lo[:, k0 + j, :]
                    ins = pe.matmul(gb[bank][:, 0:T], whi[:, slot, w], xh, start=first and j == 0, stop=False)
                    if fresh and j == 0:
                        ins.then_inc(w_free, 1)
                    pe.matmul(gb[bank][:, 0:T], whi[:, slot, w], xl, start=False, stop=False)
                    ins = pe.matmul(gb[bank][:, 0:T], wlo[:, slot, w], xh, start=False, stop=last and j == tiles - 1)
                if last:
                    ins.then_inc(g_full, 1)

            def room(L, m):
                pe.wait_ge(g_out, L * N_G + m + 1)

            def from_a(L, u, slot, m, bank):
                room(L, m)
                unit(L, u, slot, bank, ahi, alo, 0, True, True)

            def mean(L, n):
                pe.matmul(kb[0][:, 0:T], cc(C_ONE), acc[:, :], start=True, stop=True).then_inc(stat_full, 1)

            def ffn(L, p, a0, b0, n_in, n_out):
                pe.wait_ge(a_done, L * N_A + a0 + KD)
                mean(L, n_in)
                with pe.Fori(0, KF // 2) as i:
                    for s in range(RING):
                        from_a(L, U0[p + "i"] + RING * i + s, s, M0[p + "i"] + RING * i + s, s)
                with pe.Fori(0, KD // RING) as i:
                    for j in range(RING):
                        pe.wait_ge(b_done, L * N_B + b0 + KF)
                        room(L, M0[p + "o"] + RING * i + j)
                        for s in range(OUT_UNITS):
                            n = OUT_UNITS * j + s
                            unit(L, U0[p + "o"] + OUT_UNITS * RING * i + n, n % RING, j, bhi, blo, UT * s, s == 0, s == OUT_UNITS - 1,
                                 min(UT, KF - UT * s))
                pe.wait_ge(sum_done, L * N_SUM + (3 if p == "f2" else 1) * KD)
                mean(L, n_out)

            def log_l(L, t):
                n0 = CHUNKS[0][1]
                pe.wait_ge(rx_done, L * KI + t + 1)
                for c in (1, 2):
                    c0, n = CHUNKS[c]
                    dst = gb[2][:, (c - 1) * 2 * P:c * 2 * P]
                    pe.matmul(dst, lst[:, c0:c0 + n], rx[:, :, c0:c0 + n], start=True, stop=False)
                    pe.matmul(dst, identr[:, :], rep(maskr[:, 0:P], 2, 1), start=False, stop=True)
                dst = gb[3][0:n0, 0:2 * n0]
                pe.matmul(dst, lst[:, 0:n0], rx[:, :, 0:n0], start=True, stop=False)
                pe.matmul(dst, identr[0:n0, 0:n0], rep(maskr[0:n0, P:P + n0], 2, 1), start=False, stop=True)
                for h in range(2):
                    ins = pe.matmul(gb[3][:, 2 * n0:2 * n0 + T], halfr[:, h * P:(h + 1) * P], rx[0:HEAD_DIM, h, :], start=h == 0, stop=h == 1)
                ins.then_inc(l_full, 1)

            def ssd_step(L, t, q, g, last):
                kt = L * KI + t
                n0 = CHUNKS[0][1]
                pe.wait_ge(xbc_done, L * NXBC + 2 * N_GROUPS + t + 2)
                pe.wait_ge(val_in, L * N_VAL + V_Y + t + 1)
                for c, (c0, n) in enumerate(CHUNKS):
                    ins = pe.transpose(kb[0][:, c * P:(c + 1) * P], xs[:, q, c0:c0 + P], cc(C_ID))
                ins.then_inc(xt_full, 1)
                if not last:
                    pe.wait_ge(g_out, L * N_G + M0["ssd"] + 2 * t + 1 + RING)
                    unit(L, U0["ssd"] + 2 * t + 1, 2 * q + 1, 0, ahi, alo, 0, True, True)
                pe.wait_ge(xd_done, kt + 1)
                pe.wait_ge(b_done, L * N_B + KF + t)
                for c, rows in ((0, slice(SAMPLE, n0)), (1, slice(0, P)), (2, slice(0, P))):
                    ins = pe.matmul(kb[3][:, c * P:(c + 1) * P], bcur[rows, c, :], xdec[rows, c, :], start=True, stop=True)
                ins.then_inc(cs_full, 1)
                pe.wait_ge(m_done, kt + 1)
                for h in range(2):
                    ch = slice(h * HEAD_DIM, (h + 1) * HEAD_DIM)
                    for c, (c0, n) in enumerate(CHUNKS):
                        rhs = lx0[0:n0, h, :] if c == 0 else lx[:, ((c - 1) * 2 + h) * P:((c - 1) * 2 + h + 1) * P]
                        pe.matmul(kb[0][ch, c0:c0 + n], xdt[0:n, c, ch], rhs, start=True, stop=True)
                if not last:
                    pe.wait_ge(e_exp, kt + 1)
                    log_l(L, t + 1)
                if last:
                    pe.wait_ge(g_out, L * N_G + M0["ssd"] + 2 * t + 1 + RING)
                unit(L, U0["ssd"] + z_at(t, last), 3 if last else (2 * q + 2) % RING, 1, ahi, alo, 0, True, True)
                pe.wait_ge(p_done, kt + 1)
                pe.wait_ge(st_landed, 16 * (L * KI + t) + 16)
                cg = N_GROUPS + g
                for b in range(SEQS):
                    c = slice(b * STEPS, (b + 1) * STEPS)
                    pe.matmul(kb[1][:, c], st[:, b * P:(b + 1) * P], bc[:, cg, c], start=True, stop=True)
                pe.matmul(kb[1][:, SAMPLE:n0], ztile[:, :], bc[:, cg, SAMPLE:n0], start=True, stop=True)
                for c in (1, 2):
                    c0, n = CHUNKS[c]
                    ins = pe.matmul(kb[1][:, c0:c0 + n], pst[:, c - 1, :], bc[:, cg, c0:c0 + n], start=True, stop=True)
                ins.then_inc(y_full, 1)
                for b in range(SEQS):
                    ins = pe.matmul(kb[2 + b // 4][:, (b % 4) * P:(b % 4 + 1) * P], bm[:, b, :], xdec[0:SAMPLE, 0, :], start=True, stop=True)
                ins.then_inc(su_full, 1)

            with pe.Fori(0, DEPTH) as L:
                ffn(L, "f1", 0, 0, ST_F1A, ST_F1B)
                pe.wait_ge(a_done, L * N_A + 2 * KD)
                mean(L, ST_MA)
                pe.wait_ge(dtw_lo, L + 1)
                for c, (c0, n) in enumerate(CHUNKS):
                    dst = kb[1][:, c * N_HEADS:(c + 1) * N_HEADS]
                    for k in range(KD):
                        pe.matmul(dst, ahi[:, k, c0:c0 + P], dthi[:, k, :], start=k == 0, stop=False)
                        pe.matmul(dst, alo[:, k, c0:c0 + P], dthi[:, k, :], start=False, stop=False)
                        pe.matmul(dst, ahi[:, k, c0:c0 + P], dtlo[:, k, :], start=False, stop=k == KD - 1)
                    ins = pe.matmul(kb[1][:, DK + c:DK + c + 1], acc[:, c0:c0 + P], con[:, C_ONE:C_ONE + 1], start=True, stop=True)
                ins.then_inc(dt_full, 1)
                with pe.Fori(0, 2 * N_GROUPS // RING) as i:
                    for s in range(RING):
                        from_a(L, U0["bc"] + RING * i + s, s, M0["bc"] + RING * i + s, s)
                pe.wait_ge(a4_done, L + 1)
                for c, (c0, n) in enumerate(CHUNKS):
                    pe.matmul(kb[2][:, c0:c0 + n], a4[0:n, c, :, :].rearrange("p r h -> p (r h)"), cc(tri(c), n, n), start=True, stop=True)
                    pe.matmul(kb[3][:, c * N_HEADS:(c + 1) * N_HEADS], cc(C_LAT0 if c == 0 else C_LAT1, P, n), a4[0:n, c, 0, :], start=True, stop=True)
                    pe.matmul(kb[3][:, DK + c * N_HEADS:DK + (c + 1) * N_HEADS], cc(C_META if c == 0 else C_ONE, P, n), a4[0:n, c, 0, :], start=True, stop=True)
                for b in range(SEQS):
                    ins = pe.matmul(kb[3][:, 2 * DK + b * N_HEADS:2 * DK + (b + 1) * N_HEADS], con[0:SAMPLE, C_BLK + b:C_BLK + b + 1].broadcast_to([SAMPLE, P]), a4[0:SAMPLE, 0, 0, :],
                                    start=True, stop=True)
                ins.then_inc(cum_full, 1)
                from_a(L, U0["ssd"], 0, M0["ssd"], 0)
                pe.wait_ge(xbc_done, L * NXBC + 2 * N_GROUPS + 1)
                pe.wait_ge(ss_done, L + 1)
                pe.wait_ge(dec_done, L + 1)
                for g in range(N_GROUPS):
                    for c, (c0, n) in enumerate(CHUNKS):
                        ins = pe.matmul(kb[g][:, c0:c0 + n], bc[:, g, c0:c0 + P], bc[:, N_GROUPS + g, c0:c0 + n], start=True, stop=True)
                    ins.then_inc(cbt_full, 1)
                    pe.wait_ge(cbt_free, L * 2 * N_GROUPS + 2 * g + 1)
                    for c, (c0, n) in enumerate(CHUNKS):
                        ins = pe.transpose(kb[g][:, c * P:(c + 1) * P], bc[:, g, c0:c0 + P], cc(C_ID))
                    ins.then_inc(cbt_full, 1)
                pe.wait_ge(cbt_free, (L + 1) * 2 * N_GROUPS)
                log_l(L, 0)
                with pe.Fori(0, KI // 2 - 1) as i:
                    for q in range(2):
                        ssd_step(L, 2 * i + q, q, i // 2, False)
                for q in range(2):
                    ssd_step(L, KI - 2 + q, q, N_GROUPS - 1, q == 1)
                pe.wait_ge(b_done, L * N_B + KF + KI)
                mean(L, ST_Y)
                with pe.Fori(0, KD // RING) as i:
                    for j in range(RING):
                        u, m, r = U0["sbr"] + 3 * RING * i + 3 * j, M0["sbr"] + 2 * RING * i + 2 * j, 2 * (j % 2)
                        from_a(L, u, (3 * j) % RING, m, r)
                        room(L, m + 1)
                        for s in range(2):
                            unit(L, u + 1 + s, (3 * j + 1 + s) % RING, r + 1, bhi, blo, UT * s, s == 0, s == 1)
                for s in range(KD):
                    from_a(L, U0["u"] + s, s % RING, M0["u"] + s, s % RING)
                for g in range(N_GROUPS):
                    pe.wait_ge(b_done, L * N_B + KF + KI + 2 * g + 2)
                    for mm in range(2):
                        m = 2 * g + mm
                        room(L, M0["pw"] + m)
                        unit(L, U0["pw"] + g, g, m % RING, bhi, blo, 2 * g, True, True, 2, 2 * mm, mm == 0)
                with pe.Fori(0, KD // 2) as i:
                    for j in range(2):
                        from_a(L, U0["pbr"] + RING * i + 2 * j, 2 * j, M0["pbr"] + RING * i + 2 * j, 2 * j)
                        room(L, M0["pbr"] + RING * i + 2 * j + 1)
                        pe.wait_ge(b_done, L * N_B + KF + KI + 2 * KD)
                        unit(L, U0["pbr"] + RING * i + 2 * j + 1, 2 * j + 1, 2 * j + 1, bhi, blo, KD, True, True)
                with pe.Fori(0, KD // RING) as i:
                    for s in range(RING):
                        pe.wait_ge(b_done, L * N_B + KF + KI + 3 * KD)
                        room(L, M0["wo"] + RING * i + s)
                        unit(L, U0["wo"] + RING * i + s, s, s, bhi, blo, 0, True, True)
                pe.wait_ge(sum_done, L * N_SUM + 2 * KD)
                mean(L, ST_MB)
                ffn(L, "f2", 2 * KD, KF + KI + 3 * KD, ST_F2A, ST_F2B)


def kernel(**inputs):
    import numpy as np
    import concourse.bacc as bacc
    from concourse.bass_utils import run_bass_kernel_spmd

    f = {k: np.ascontiguousarray(v) for k, v in inputs.items()}

    def tiles(w):
        d, k, m = w.shape
        return w.reshape(d, k // P, P, m // P, P).transpose(0, 1, 3, 2, 4)

    wts = np.zeros((DEPTH, UNITS, UT, P, P), np.float32)
    zxbc = np.ascontiguousarray(f["w_in"][:, :, :D_INNER + (KI + 2 * N_GROUPS) * P])
    rest = np.ascontiguousarray(f["w_in"][:, :, D_INNER + NXBC * P + N_HEADS:])
    zx, ug = tiles(zxbc), tiles(rest)
    for p, n in (("f1", "ffn1"), ("f2", "ffn2")):
        wi, wo = tiles(f[n + "_w_in"]), tiles(f[n + "_w_out"])
        for j in range(KF):
            wts[:, U0[p + "i"] + 2 * j] = wi[:, :, j]
            wts[:, U0[p + "i"] + 2 * j + 1] = wi[:, :, KF + j]
        for m in range(KD):
            for s in range(OUT_UNITS):
                part = wo[:, UT * s:UT * (s + 1), m]
                wts[:, U0[p + "o"] + OUT_UNITS * m + s, :part.shape[1]] = part
    for c in range(2 * N_GROUPS):
        wts[:, U0["bc"] + c] = zx[:, :, 2 * KI + c]
    for t in range(KI):
        wts[:, U0["ssd"] + (2 * t - 1 if t else 0)] = zx[:, :, KI + t]
        wts[:, U0["ssd"] + z_at(t, t == KI - 1)] = zx[:, :, t]
    sbr, pbr, wo = tiles(f["w_ssd_branch"]), tiles(f["w_pool_branch"]), tiles(f["w_out"])
    for m in range(KD):
        wts[:, U0["sbr"] + 3 * m] = ug[:, :, KD + m]
        wts[:, U0["sbr"] + 3 * m + 1] = sbr[:, :UT, m]
        wts[:, U0["sbr"] + 3 * m + 2] = sbr[:, UT:, m]
        wts[:, U0["u"] + m] = ug[:, :, m]
        wts[:, U0["pbr"] + 2 * m] = ug[:, :, 2 * KD + m]
        wts[:, U0["pbr"] + 2 * m + 1] = pbr[:, :, m]
        wts[:, U0["wo"] + m] = wo[:, :, m]
    for g in range(N_GROUPS):
        pw = tiles(f["pool_w"][:, g])
        for mm in range(2):
            wts[:, U0["pw"] + g, 2 * mm:2 * mm + 2] = pw[:, :, mm]
    wts = np.ascontiguousarray(wts.transpose(0, 1, 3, 2, 4)).reshape(DEPTH * UNITS, P, UT * P)

    def cols(v, n):
        return v.reshape(DEPTH, n, P).transpose(2, 0, 1)

    def conv_order(v):
        return np.concatenate([v[..., D_INNER:], v[..., :D_INNER]], axis=-1)

    par = np.zeros((P, DEPTH, NPAR), np.float32)
    for at, n in ((G_F1A, "ln_ffn1_pre"), (G_F1B, "ln_ffn1_post"), (G_MA, "ln_mix_pre"), (G_MB, "ln_mix_post"),
                  (G_F2A, "ln_ffn2_pre"), (G_F2B, "ln_ffn2_post"), (G_PS, "pool_scale")):
        par[:, :, at:at + KD] = cols(f[n], KD)
    par[:, :, G_SSD:G_SSD + KI] = cols(f["ssd_norm"], KI)
    par[:, :, G_D:G_D + KI] = cols(np.repeat(f["d_skip"], HEAD_DIM, axis=1), KI)
    par[:, :, G_CB:G_CB + NXBC] = cols(conv_order(f["conv_b"]), NXBC)
    for k in range(CONV_K):
        par[:, :, G_CW + k:G_CW + CONV_K * NXBC:CONV_K] = cols(conv_order(f["conv_w"][:, k]), NXBC)
    par[:, :, G_DTB:G_DTB + N_HEADS] = f["dt_bias"][None]
    par[:, :, G_AL:G_AL + N_HEADS] = f["a_log"][None]

    con = np.zeros((P, NCON), np.float32)
    ar = np.arange(P)
    seq = np.where(ar < SAMPLE, ar // STEPS, SEQS)
    same = seq[:, None] == seq[None, :]
    before = ar[:, None] <= ar[None, :]
    real = (ar < CHUNKS[0][1])
    con[:, C_ID:C_ID + P] = np.eye(P)
    con[:, C_TRI1:C_TRI1 + P] = before
    con[:, C_TRI0:C_TRI0 + P] = before & same
    con[:, C_LAT1:C_LAT1 + P] = ~before
    con[:, C_LAT0:C_LAT0 + P] = ~before & same & real[None, :]
    con[:, C_ONE:C_ONE + P] = 1
    con[SAMPLE:CHUNKS[0][1], C_META:C_META + P] = 1
    own = np.zeros((P, 4 * P), np.float32)
    own[:, 0:P] = np.where(before, 0, MASKED)
    own[:, P:2 * P] = np.where(before & same, 0, MASKED)
    own[:, 2 * P:2 * P + HEAD_DIM] = 1
    own[:, 3 * P + HEAD_DIM:] = 1
    con[:, C_SEL:C_SEL + N_HEADS] = (ar % N_HEADS)[:, None] == np.arange(N_HEADS)
    con[:SAMPLE, C_BLK:C_BLK + SEQS] = (ar[:SAMPLE] // STEPS)[:, None] == np.arange(SEQS)
    for w in range(4):
        win = 2 << w
        con[:, C_CNT + w * PHIST:C_CNT + (w + 1) * PHIST] = win / np.minimum(np.arange(PHIST) + 1, win)

    tokens = np.concatenate([f["x_sample"].reshape(SAMPLE, D_MODEL), f["meta_tokens"], f["x_prompt"][0]])
    arrays = {
        "x_in": tokens.T.reshape(KD, P, T).transpose(1, 0, 2),
        "wts": wts,
        "par_in": par,
        "con_in": con,
        "own_dram": own,
        "dtw_in": f["w_in"][:, :, D_INNER + NXBC * P:D_INNER + NXBC * P + N_HEADS].reshape(DEPTH, KD, P, N_HEADS).transpose(0, 2, 1, 3),
        "cst_in": conv_order(f["state_conv"]).reshape(DEPTH, SEQS * HIST, NXBC, P).transpose(0, 3, 2, 1),
        "pst_in": f["state_pool"].reshape(DEPTH, SEQS * PHIST, KD, P).transpose(0, 3, 2, 1),
        "ssm_in": f["state_ssm"].reshape(DEPTH, SEQS, KI, P, D_STATE).transpose(0, 2, 4, 1, 3).reshape(DEPTH * KI, P, SEQS * P),
    }
    outs = {"y": (P, KD, T), "ssm_o": (DEPTH * KI, P, SO), "conv_o": (DEPTH * NXBC, P, CKEEP), "pool_o": (DEPTH, P, KD, PKEEP)}
    nc = bacc.Bacc("TRN2", target_bir_lowering=False, num_devices=1)
    arrays = {k: np.ascontiguousarray(v) for k, v in arrays.items()}
    aps = [nc.dram_tensor(k, v.shape, F32, kind="ExternalInput").ap() for k, v in arrays.items()]
    aps += [nc.dram_tensor(k, s, F32, kind="ExternalOutput").ap() for k, s in outs.items()]
    build(nc, *aps)
    got = run_bass_kernel_spmd(nc, [arrays], core_ids=[0]).results[0]

    y = got["y"].transpose(1, 0, 2).reshape(D_MODEL, T).T
    s = got["ssm_o"].reshape(DEPTH, KI, D_STATE, SEQS + 1, P).transpose(3, 0, 1, 4, 2).reshape(SEQS + 1, DEPTH, N_HEADS, HEAD_DIM, D_STATE)
    c = got["conv_o"].reshape(DEPTH, NXBC * P, SEQS + 1, HIST).transpose(0, 2, 3, 1)
    c = np.concatenate([c[..., 2 * N_GROUPS * P:], c[..., :2 * N_GROUPS * P]], axis=-1)
    p = got["pool_o"].transpose(0, 2, 1, 3).reshape(DEPTH, D_MODEL, SEQS + 1, PHIST).transpose(0, 2, 3, 1)
    return tuple(np.ascontiguousarray(v) for v in (
        y[SAMPLE + N_META:].reshape(1, SEQ, D_MODEL), y[:SAMPLE].reshape(SEQS, STEPS, D_MODEL),
        s[SEQS:].transpose(1, 0, 2, 3, 4), c[:, SEQS:], p[:, SEQS:],
        s[:SEQS].transpose(1, 0, 2, 3, 4), c[:, :SEQS], p[:, :SEQS]))
```

```python
from contextlib import ExitStack

import concourse.bass as bass
from concourse import mybir
from concourse.alu_op_type import AluOpType as ALU

ACT = mybir.ActivationFunctionType
F32 = mybir.dt.float32
F32R = mybir.dt.float32r

P = 128
D_MODEL, D_FF, D_INNER, DEPTH = 1024, 2816, 2048, 2
N_HEADS, HEAD_DIM, N_GROUPS, D_STATE = 32, 64, 4, 128
SEQS, STEPS, N_META, SEQ = 8, 8, 16, 256
CONV_K, MAX_WIN = 4, 16
EPS = 1e-6

KD, KF, KI = D_MODEL // P, D_FF // P, D_INNER // P
SAMPLE = SEQS * STEPS
T = SAMPLE + N_META + SEQ
CHUNKS = [(0, SAMPLE + N_META), (SAMPLE + N_META, P), (SAMPLE + N_META + P, P)]
NXBC = KI + 2 * N_GROUPS
HIST = CONV_K - 1
CSTRIDE = STEPS + HIST
CW = SEQS * CSTRIDE + HIST + N_META + SEQ
CP = SEQS * CSTRIDE
PHIST = MAX_WIN - 1
PSTRIDE = STEPS + PHIST
PW = SEQS * PSTRIDE + PHIST + N_META + SEQ
PP = SEQS * PSTRIDE
CKEEP = HIST * (SEQS + 1)
PKEEP = PHIST * (SEQS + 1)

UT = 8
RING = 4
OUT_UNITS = 3
AHEAD = 2

G_F1A, G_F1B, G_MA, G_MB, G_F2A, G_F2B = (KD * i for i in range(6))
G_SSD = 6 * KD
G_D = G_SSD + KI
G_PS = G_D + KI
G_CB = G_PS + KD
G_CW = G_CB + NXBC
G_DTB = G_CW + CONV_K * NXBC
G_AL = G_DTB + N_HEADS
NPAR = G_AL + N_HEADS

C_ID = 0
C_TRI1 = C_ID + P
C_TRI0 = C_TRI1 + P
C_LAT1 = C_TRI0 + P
C_LAT0 = C_LAT1 + P
C_ONE = C_LAT0 + P
C_META = C_ONE + P
C_SEL = C_META + P
C_BLK = C_SEL + N_HEADS
C_CNT = C_BLK + SEQS
NCON = C_CNT + 4 * PHIST

N_G = 2 * (2 * KF + KD) + 1 + 2 * N_GROUPS + 2 * KI + 3 * KD + KD + 2 * KD + KD
N_A = 3 * KD
N_B = 2 * KF + KI + 3 * KD
N_HI = N_A + N_B
N_VAL = 2 * KF + KI + 5 * KD
N_GATE = 2 * KF + KI + 2 * KD
N_SQ = 3 * KD + 3 * KD + KI
N_SUM = 3 * KD
N_XSUM = 3 * (KD - 1)
N_STAT = 7
N_PBT = 2

ST_F1A, ST_F1B, ST_MA, ST_Y, ST_MB, ST_F2A, ST_F2B = range(N_STAT)

V_F1, V_X1, V_Y = KD, KD + KF, 2 * KD + KF
V_U = V_Y + KI
V_MG, V_X2, V_F2 = V_U + KD, V_U + 2 * KD, V_U + 3 * KD
H_F1, H_X1, H_Y = KD, KD + KF, 2 * KD + KF
H_U = H_Y + KI
H_PW, H_MG, H_X2, H_F2 = (H_U + KD * i for i in range(1, 5))
S_F1, S_X1, S_Y = KD, 2 * KD, 3 * KD
S_WO, S_X2, S_F2 = (S_Y + KI + KD * i for i in range(3))
MASKED = -30000.0

PW_UNITS = (2, 1, 1)
PHASES = {
    "f1i": (2 * KF, 2 * KF), "f1o": (OUT_UNITS * KD, KD), "dt": (1, 1), "bc": (2 * N_GROUPS, 2 * N_GROUPS),
    "ssd": (2 * KI, 2 * KI), "mix": (4 * KD, 3 * KD), "pw": (len(PW_UNITS), KD),
    "pbr": (2 * KD, 2 * KD), "wo": (KD, KD), "f2i": (2 * KF, 2 * KF), "f2o": (OUT_UNITS * KD, KD),
}
U0, M0 = {}, {}
UNITS = N_M = 0
for _name, (_u, _m) in PHASES.items():
    U0[_name], M0[_name] = UNITS, N_M
    UNITS, N_M = UNITS + _u, N_M + _m
assert N_M == N_G and UNITS % RING == 0 and SEQS == UT

def z_at(t, last):
    return 2 * t + (1 if last else 2)


def slot_of(phase, n):
    return (U0[phase] + n) % RING


TILES_PER_GROUP = KI // N_GROUPS

XS_BANK, Z_BANK = 1, 0
U_BANK, GATE_BANK, SB_BANK = 1, 2, 3

SO = SEQS * P + P
DK = 3 * N_HEADS


def rep(ap, n, at):
    v = ap.unsqueeze(at)
    shape = list(v.shape)
    shape[at] = n
    return v.broadcast_to(shape)


def seqs(ap, stride):
    return ap.rearrange("p (b s) -> p b s", s=stride)


def build(nc, x_in, wts, par_in, con_in, own_dram, cst_in, pst_in, ssm_in, y_out, ssm_out, conv_out, pool_out):
    with ExitStack() as ctx:
        def sb(name, shape, dt=F32):
            return ctx.enter_context(nc.sbuf_tensor(name, shape, dt))

        def sem(name):
            return ctx.enter_context(nc.semaphore(name))

        align = 32
        b_at = -(-nc.sbuf_base // align) * align
        bhi = sb("bhi", [P, KF, T], F32R)
        blo = sb("blo", [P, KF, T], F32R)
        tail_at = [b_at + KI * T * 4, b_at + (KF + KI) * T * 4]
        tail = [nc.alloc_sbuf_tensor_at(f"tail{i}", [P, (KF - KI) * T], F32, offset=o) for i, o in enumerate(tail_at)]
        x = sb("x", [P, KD, T])
        ahi = sb("ahi", [P, KD, T], F32R)
        alo = sb("alo", [P, KD, T], F32R)
        wraw = sb("wraw", [P, RING, UT * P])
        whi = sb("whi", [P, RING, UT * P], F32R)
        wlo = sb("wlo", [P, RING, UT * P], F32R)
        fo = sb("fo", [P, KD, T])
        bc = sb("bc", [P, 2 * N_GROUPS, T])
        par = sb("par", [P, DEPTH, NPAR])
        con = sb("con", [P, NCON])
        maskr = sb("maskr", [P, 2 * P], F32R)
        identr = sb("identr", [P, P], F32R)
        halfr = sb("halfr", [HEAD_DIM, 2 * P], F32R)
        eps = sb("eps", [P, 2])
        acc = sb("acc", [P, T])
        rpre = sb("rpre", [P, T])
        rpost = sb("rpost", [P, T])
        t_a = sb("t_a", [P, RING, T])
        t_b = sb("t_b", [P, RING, T])
        sq = sb("sq", [P, RING, T])
        xp = sb("xp", [P, CW])
        cv = sb("cv", [P, CW - HIST])
        cst = sb("cst", [P, NXBC, SEQS * HIST])
        cso = sb("cso", [P, 2, CKEEP])
        ea = sb("ea", [P, N_HEADS])
        ss = sb("ss", [P, T], F32R)
        lst = sb("lst", [P, T], F32R)
        dec = sb("dec", [P, 2 * DK + SEQS * N_HEADS])
        rx = sb("rx", [P, 2, T], F32R)
        ztile = sb("ztile", [P, P])
        st = sb("st", [P, SEQS * P])
        pfin = sb("pfin", [P, P])
        eab = sb("eab", [P, 2, T])

        class Carve:
            def __init__(self, ap):
                self.ap, self.at = ap, 0

            def take(self, *shape, rows=P):
                n = 1
                for d in shape:
                    n *= d
                v = self.ap[0:rows, self.at:self.at + n]
                self.at += n
                if len(shape) > 1:
                    names = "abc"[:len(shape)]
                    v = v.rearrange(f"p ({' '.join(names)}) -> p {' '.join(names)}", **dict(zip(names, shape)))
                return v

        def flat(t):
            return t[:, :, :].rearrange("p a b -> p (a b)")

        c = Carve(flat(fo))
        cb = c.take(N_GROUPS, T)
        pst = c.take(2, P)
        bm = c.take(SEQS, P, rows=SAMPLE)
        c = Carve(flat(sq))
        sp = c.take(6, DK)
        a4 = c.take(3, 4, N_HEADS)
        c = Carve(flat(sq)[:, T:])
        lx = c.take(4 * P)
        lx0 = c.take(2, CHUNKS[0][1])
        xs = t_b[:, 2:4, :]
        c = Carve(tail[0][:, :])
        bt = c.take(N_GROUPS, 3, P)
        bcur = c.take(3, P)
        c = Carve(tail[0][:, :])
        ph = c.take(KD, SEQS * PHIST)
        up = [c.take(PW) for _ in range(2)]
        c = Carve(tail[1][:, :])
        so = c.take(SO)
        xdt = c.take(3, P)
        xdec = c.take(3, P)
        dt = c.take(3, N_HEADS)
        pso = Carve(tail[1][:, :]).take(KD, PKEEP)
        win = [flat(sq)[:, i * PW:(i + 1) * PW] for i in range(2)]
        pooled = bc
        own_in = flat(t_a)[:, 0:4 * P]

        gb = [ctx.enter_context(nc.psum_tensor(f"gb{i}", [P, 512], F32)) for i in range(RING)]
        kb = [ctx.enter_context(nc.psum_tensor(f"kb{i}", [P, 512], F32)) for i in range(4)]

        s_x = [sem(f"x_landed{i}") for i in range(2)]
        s_con = sem("constants_landed")
        s_eps = sem("eps_ready")
        s_hist = sem("histories_landed")
        s_hfree = sem("histories_used")
        w_landed = [sem(f"w_landed{i}") for i in range(RING)]
        w_rawfree = sem("w_raw_free")
        w_hi = sem("w_hi_ready")
        w_lo = sem("w_lo_ready")
        w_free = sem("w_free")
        g_full = sem("gemm_bank_full")
        g_out = sem("gemm_bank_evicted")
        a_done = sem("a_tile_ready")
        b_done = sem("b_tile_ready")
        hi_done = sem("hi_part_ready")
        gate_done = sem("gate_ready")
        val_in = sem("value_ready")
        sum_done = sem("square_of_output_summed")
        sq_done = sem("square_ready")
        stat_full = sem("mean_square_ready")
        sd_done = sem("rms_ready")
        consts = sem("constants_ready")
        cv_in = sem("conv_sum_ready")
        xbc_done = sem("xbc_tile_ready")
        dt_raw = sem("dt_product_scaled")
        dt_full = sem("dt_token_major")
        x_sum = sem("square_of_x_summed")
        dt_a = sem("dt_step_for_act")
        dt_b = sem("dt_step_by_act")
        a4_done = sem("log_decays_ready")
        cum_full = sem("cumulated_ready")
        dec_done = sem("decays_ready")
        ss_done = sem("cumulated_split")
        bt_full = sem("bt_full")
        bt_free = sem("bt_evicted")
        cb_full = sem("cb_full")
        cb_free = sem("cb_evicted")
        rx_done = sem("head_rows_ready")
        l_full = sem("log_l_ready")
        l_exp = sem("l_ready")
        e_exp = sem("decay_per_channel_ready")
        st_dec = sem("states_decayed")
        xt_full = sem("x_transposed")
        xd_done = sem("xdt_ready")
        b_ready = sem("group_b_in_place")
        bm_ready = sem("group_b_apart")
        m_done = sem("masked_cb_ready")
        cs_full = sem("chunk_states_ready")
        p_done = sem("states_chained")
        y_full = sem("y_products_ready")
        y_read = sem("y_products_read")
        su_full = sem("sample_update_ready")
        so_done = sem("new_states_ready")
        so_free = sem("new_states_stored")
        st_landed = sem("states_landed")
        s_ph = sem("pool_history_landed")
        cso_done = sem("conv_rows_staged")
        cso_free = [sem(f"conv_rows_stored{i}") for i in range(2)]
        pso_done = sem("pool_rows_staged")
        pso_free = sem("pool_rows_stored")
        s_out = sem("y_stored")

        def cc(c, n=P, rows=P):
            return con[0:rows, c:c + n]

        def tri(c):
            return (C_TRI0 if c == 0 else C_TRI1)

        block = ctx.enter_context(nc.Block())

        @block.sync
        def _(sp_):
            def unit(u, slot):
                sp_.wait_ge(w_rawfree, u + 1)
                sp_.dma_start(wraw[:, slot, :], wts[u, :, :]).then_inc(w_landed[slot], 16)

            def units(L, u0, u1):
                with sp_.Fori(u0 // RING, u1 // RING) as i:
                    for s in range(RING):
                        unit(L * UNITS + RING * i + s, s)

            with sp_.Fori(0, DEPTH) as L:
                units(L, 0, U0["f1o"])
                sp_.wait_ge(s_hfree, L + 1)
                sp_.dma_start(cst[:, :, :], cst_in[L, :, :, :]).then_inc(s_hist, 16)
                units(L, U0["f1o"], UNITS)
            for s in range(AHEAD):
                sp_.wait_ge(w_rawfree, DEPTH * UNITS + s + 1)
                sp_.dma_start(wraw[:, s, :], wts[s, :, :]).then_inc(w_landed[s], 16)

        @block.gpsimd
        def _(pool):
            pool.sem_inc(w_rawfree, RING)

            def lo(u, s):
                pool.wait_ge(w_hi, u + 1)
                pool.tensor_tensor(wlo[:, s, :], wraw[:, s, :], whi[:, s, :].bitcast(F32), ALU.subtract).then_inc(w_lo, 1)
                pool.wait_ge(w_lo, u + 1)
                pool.sem_inc(w_rawfree, 1)

            def ahead(L, u):
                lo(L * UNITS + u + AHEAD, (u + AHEAD) % RING)

            def run(L, u0, u1):
                n = (u1 - u0) // RING
                with pool.Fori(0, n) as i:
                    for s in range(RING):
                        lo(L * UNITS + u0 + AHEAD + RING * i + s, (u0 + AHEAD + s) % RING)
                for u in range(u0 + n * RING, u1):
                    ahead(L, u)

            def sum_x(L, u, n, s0):
                ahead(L, u)
                for k in range(1, KD):
                    pool.wait_ge(sq_done, L * N_SQ + s0 + k + 1)
                    if k == 1:
                        pool.tensor_tensor(acc[:, :], sq[:, 0, :], sq[:, 1, :], ALU.add).then_inc(x_sum, 1)
                        ahead(L, u + 1)
                    else:
                        pool.wait_ge(x_sum, L * N_XSUM + n * (KD - 1) + k - 1)
                        pool.tensor_tensor(acc[:, :], acc[:, :], sq[:, k % RING, :], ALU.add).then_inc(x_sum, 1)

            def ssd_step(L, t, q, last):
                u = U0["ssd"] + 2 * t
                if not last:
                    lo(L * UNITS + u + 1 + AHEAD, slot_of("ssd", 2 * q + 1 + AHEAD))
                pool.wait_ge(dec_done, L + 1)
                pool.wait_ge(st_landed, 16 * (L * KI + t) + 16)
                pool.wait_ge(so_free, 16 * (L * KI + t) + 16)
                ds_ = dec[:, 2 * DK:].rearrange("p (b h) -> p b h", b=SEQS)[:, :, bass.ds(2 * t, 2)]
                pool.tensor_tensor(so[:, 0:SEQS * P].rearrange("p (b h d) -> p b h d", b=SEQS, h=2),
                                   st[:, :].rearrange("p (b h d) -> p b h d", b=SEQS, h=2), rep(ds_, HEAD_DIM, 3), ALU.mult).then_inc(st_dec, 1)
                lo(L * UNITS + U0["ssd"] + z_at(t, last) + AHEAD, slot_of("ssd", z_at(q + 2, last) + AHEAD))

            for s in range(AHEAD):
                lo(s, s)
            pool.wait_ge(s_con, 32)
            pool.tensor_copy(maskr[:, :], own_in[:, 0:2 * P])
            pool.tensor_copy(identr[:, :], cc(C_ID))
            pool.tensor_copy(halfr[:, :], own_in[0:HEAD_DIM, 2 * P:4 * P]).then_inc(consts, 1)
            with pool.Fori(0, DEPTH) as L:
                sum_x(L, 0, 0, 0)
                run(L, 2, U0["dt"])
                sum_x(L, U0["dt"], 1, S_X1)
                run(L, U0["dt"] + 2, U0["ssd"] + 1)
                with pool.Fori(0, N_GROUPS - 1) as g:
                    for j in range(TILES_PER_GROUP):
                        ssd_step(L, TILES_PER_GROUP * g + j, j % 2, False)
                for j in range(TILES_PER_GROUP):
                    ssd_step(L, KI - TILES_PER_GROUP + j, j % 2, j == TILES_PER_GROUP - 1)
                run(L, U0["mix"], U0["f2i"])
                sum_x(L, U0["f2i"], 2, S_X2)
                run(L, U0["f2i"] + 2, UNITS)

        @block.scalar
        def _(act):
            act.sem_inc(xbc_done, 1)
            def load_x(half):
                k = slice(KD // 2 * half, KD // 2 * (half + 1))
                act.dma_start(x[:, k, :], x_in[:, k, :]).then_inc(s_x[half], 16)

            load_x(0)
            act.dma_start(par[:, :, :], par_in).then_inc(s_x[0], 16)

            def split(u, slot):
                act.wait_ge(w_free, u + 1)
                act.activation(whi[:, slot, :], wraw[:, slot, :], ACT.Copy).then_inc(w_hi, 1)

            def ahead(L, phase, n, step=0):
                slot = slot_of(phase, n + AHEAD)
                u = L * UNITS + step + (U0[phase] + n + AHEAD)
                at = L * (UNITS // RING * 16) + step * (16 // RING) + (U0[phase] + n + AHEAD - slot) * (16 // RING) + 16
                act.wait_ge(w_landed[slot], at)
                split(u, slot)

            def root(L, n):
                act.wait_ge(stat_full, L * N_STAT + n + 1)
                e = 1 if n in (ST_F1B, ST_F2B) else 0
                scale = (4.0 if e else 1.0) / (D_INNER if n == ST_Y else D_MODEL)
                act.activation(kb[0][:, 0:T], kb[0][:, 0:T], ACT.Sqrt, bias=eps[:, e:e + 1], scale=scale).then_inc(sd_done, 1)

            def split_x(L, gain, n, v0, phase):
                ahead(L, phase, 0)
                for k in range(KD):
                    act.wait_ge(val_in, L * N_VAL + v0 + k + 1)
                    act.activation(ahi[:, k, :], x[:, k, :], ACT.Copy, scale=par[:, L, gain + k:gain + k + 1]).then_inc(hi_done, 1)
                    if k >= RING:
                        act.wait_ge(x_sum, L * N_XSUM + n * (KD - 1) + max(1, k - RING))
                    act.activation(sq[:, k % RING, :], x[:, k, :], ACT.Square).then_inc(sq_done, 1)
                    if k == 1:
                        ahead(L, phase, 1)

            def ffn_in(L, ph_, v0):
                m0 = M0[ph_]

                def group(i, first):
                    for q in range(2):
                        if not (first and q == 0):
                            ahead(L, ph_, 2 * q, RING * i)
                        act.wait_ge(g_out, L * N_G + m0 + RING * i + 2 * q + 1 + RING)
                        act.activation(t_b[:, 2 * q, :], t_a[:, 2 * q, :], ACT.Silu).then_inc(gate_done, 1)
                        if not (first and q == 0):
                            ahead(L, ph_, 2 * q + 1, RING * i)
                        act.wait_ge(val_in, L * N_VAL + v0 + 2 * i + q + 1)
                        act.activation(bhi[:, 2 * i + q, :], t_b[:, 2 * q + 1, :], ACT.Copy).then_inc(hi_done, 1)

                group(0, True)
                with act.Fori(1, KF // 2) as i:
                    group(i, False)

            def out_squares(L, ph_, units):
                with act.Fori(0, KD // RING) as i:
                    for j in range(RING):
                        for s in range(units):
                            ahead(L, ph_, units * j + s, RING * units * i)
                        act.wait_ge(g_out, L * N_G + M0[ph_] + RING * i + j + 1 + RING)
                        act.activation(sq[:, j, :], fo[:, RING * i + j, :], ACT.Square).then_inc(sq_done, 1)

            def silu_xbc(L, c, dst, side):
                act.wait_ge(cso_done, L * NXBC + c + 1)
                act.dma_start(conv_out[L * NXBC + c, :, :], cso[:, side, :]).then_inc(cso_free[side], 16)
                act.wait_ge(cv_in, L * NXBC + c + 1)
                bias = par[:, L, bass.ds(G_CB + c, 1)]
                act.activation(seqs(dst[:, 0:SAMPLE], STEPS), seqs(cv[:, 0:CP], CSTRIDE)[:, :, 0:STEPS], ACT.Silu, bias=bias)
                act.activation(dst[:, SAMPLE:T], cv[:, CP:CW - HIST], ACT.Silu, bias=bias).then_inc(xbc_done, 1)

            def head_rows(L, t):
                for h in range(2):
                    ins = act.activation(rx[:, h, :], ss[:, :].bitcast(F32), ACT.Copy, scale=con[:, bass.ds(C_SEL + 2 * t + h, 1)])
                ins.then_inc(rx_done, 1)

            def exp_l(L, t):
                act.wait_ge(l_full, L * KI + t + 1)
                act.activation(lx, gb[2][:, :], ACT.Exp)
                n0 = CHUNKS[0][1]
                act.activation(lx0[0:n0, :, :].rearrange("p a b -> p (a b)"), gb[3][0:n0, 0:2 * n0], ACT.Exp).then_inc(l_exp, 1)

            def exp_e(q):
                act.activation(eab[:, q, :], gb[3][:, 2 * CHUNKS[0][1]:2 * CHUNKS[0][1] + T], ACT.Exp).then_inc(e_exp, 1)

            def ssd_step(L, t, q, last):
                if not last:
                    head_rows(L, t + 1)
                    ahead(L, "ssd", 1 + 2 * q, 2 * t - 2 * q)
                    exp_l(L, t + 1)
                    exp_e(1 - q)
                    silu_xbc(L, 2 * N_GROUPS + t + 1, xs[:, 1 - q, :], 1 - q)
                z = z_at(t, last)
                ahead(L, "ssd", z_at(q, last), 2 * t - 2 * q)
                act.wait_ge(g_out, L * N_G + M0["ssd"] + z + 1 + RING)
                act.activation(t_b[:, 0, :], t_b[:, 1, :], ACT.Silu).then_inc(gate_done, 1)
                act.wait_ge(val_in, L * N_VAL + V_Y + t + 1)
                act.activation(bhi[:, t, :], t_a[:, 3, :], ACT.Copy, scale=par[:, L, bass.ds(G_SSD + t, 1)]).then_inc(hi_done, 1)
                act.activation(sq[:, 0, :], t_a[:, 3, :], ACT.Square).then_inc(sq_done, 1)
                if not last:
                    act.wait_ge(st_dec, L * KI + t + 1)
                    load_states(L, t + 1)
                act.wait_ge(so_done, L * KI + t + 2)
                act.dma_start(ssm_out[L * KI + t, :, :], so).then_inc(so_free, 16)

            def load_states(L, t):
                act.dma_start(st[:, :], ssm_in[L * KI + t, :, :]).then_inc(st_landed, 16)

            def evict_bt(L, g):
                act.wait_ge(bt_full, L * N_GROUPS + g + 1)
                act.activation(bt[:, g, :, :].rearrange("p c n -> p (c n)"), kb[g % 2][:, 0:3 * P], ACT.Copy).then_inc(bt_free, 1)

            for s in range(AHEAD):
                act.wait_ge(w_landed[s], 16)
                split(s, s)
                if s == 0:
                    load_x(1)
            act.dma_start(con[:, :], con_in).then_inc(s_con, 16)
            act.dma_start(own_in, own_dram).then_inc(s_con, 16)
            act.wait_ge(s_eps, 1)
            with act.Fori(0, DEPTH) as L:
                split_x(L, G_F1A, 0, 0, "f1i")
                root(L, ST_F1A)
                ffn_in(L, "f1i", V_F1)
                out_squares(L, "f1o", OUT_UNITS)
                root(L, ST_F1B)
                split_x(L, G_MA, 1, V_X1, "dt")
                root(L, ST_MA)
                act.wait_ge(s_hist, (L + 1) * 16)
                for c in range(2 * N_GROUPS):
                    ahead(L, "dt", c + 2)
                    if c == 1:
                        act.activation(ea[:, :], par[:, L, G_AL:G_AL + N_HEADS], ACT.Exp)
                        act.wait_ge(dt_a, L * 2 + 1)
                        act.activation(sp[:, 2, :], sp[:, 1, :], ACT.Exp, scale=-1.0).then_inc(dt_b, 1)
                    if c == 2:
                        act.wait_ge(dt_a, L * 2 + 2)
                        act.activation(sp[:, 4, :], sp[:, 3, :], ACT.Ln).then_inc(dt_b, 1)
                    if c == 2 * N_GROUPS - 1:
                        act.wait_ge(cum_full, L + 1)
                        act.activation(dec[:, :], kb[3][:, 0:2 * DK + SEQS * N_HEADS], ACT.Exp).then_inc(dec_done, 1)
                    silu_xbc(L, c, bc[:, c, :], c % 2)
                    if c >= N_GROUPS:
                        evict_bt(L, c - N_GROUPS)
                silu_xbc(L, 2 * N_GROUPS, xs[:, 0, :], 0)
                act.wait_ge(ss_done, L + 1)
                load_states(L, 0)
                head_rows(L, 0)
                exp_l(L, 0)
                exp_e(0)
                with act.Fori(0, N_GROUPS - 1) as g:
                    for j in range(TILES_PER_GROUP):
                        ssd_step(L, TILES_PER_GROUP * g + j, j % 2, False)
                for j in range(TILES_PER_GROUP):
                    ssd_step(L, KI - TILES_PER_GROUP + j, j % 2, j == TILES_PER_GROUP - 1)
                act.dma_start(ph, pst_in[L, :, :, :]).then_inc(s_ph, 16)

                def gate(m, first):
                    ahead(L, "mix", 0, 4 * m)
                    ahead(L, "mix", 1, 4 * m)
                    if first:
                        root(L, ST_Y)
                    ahead(L, "mix", 2, 4 * m)
                    act.wait_ge(g_out, L * N_G + M0["mix"] + 3 * m + 2 + RING)
                    act.activation(t_b[:, 0, :], t_a[:, 0, :], ACT.Sigmoid).then_inc(gate_done, 1)
                    ahead(L, "mix", 3, 4 * m)

                gate(0, True)
                with act.Fori(1, KD) as m:
                    gate(m, False)
                act.wait_ge(pso_done, L + 1)
                act.dma_start(pool_out[L, :, :, :], pso).then_inc(pso_free, 16)
                act.wait_ge(g_full, L * N_G + M0["pw"])
                for k in range(KD):
                    act.wait_ge(val_in, L * N_VAL + V_U + k + 1)
                    act.activation(bhi[:, k, :], pooled[:, k, :], ACT.Copy).then_inc(hi_done, 1)
                g = 0
                for n, groups in enumerate(PW_UNITS):
                    ahead(L, "pw", n)
                    for m in range(2 * g, 2 * (g + groups)):
                        act.wait_ge(g_full, L * N_G + M0["pw"] + m + 1)
                        act.activation(bhi[:, KD + m, :], gb[m % RING][:, 0:T], ACT.Copy,
                                       scale=par[:, L, G_PS + m:G_PS + m + 1]).then_inc(hi_done, 1)
                    g += groups
                with act.Fori(0, KD // 2) as i:
                    for j in range(2):
                        ahead(L, "pbr", 2 * j, RING * i)
                        act.wait_ge(g_out, L * N_G + M0["pbr"] + RING * i + 2 * j + 1 + RING)
                        act.activation(t_b[:, 2 * j, :], t_a[:, 2 * j, :], ACT.Sigmoid).then_inc(gate_done, 1)
                        ahead(L, "pbr", 2 * j + 1, RING * i)
                        act.wait_ge(val_in, L * N_VAL + V_MG + 2 * i + j + 1)
                        act.activation(bhi[:, 2 * i + j, :], t_b[:, 2 * j + 1, :], ACT.Copy).then_inc(hi_done, 1)
                out_squares(L, "wo", 1)
                root(L, ST_MB)
                split_x(L, G_F2A, 2, V_X2, "f2i")
                root(L, ST_F2A)
                ffn_in(L, "f2i", V_F2)
                out_squares(L, "f2o", OUT_UNITS)
                root(L, ST_F2B)
            for half in range(2):
                act.wait_ge(val_in, DEPTH * N_VAL + KD // 2 * (half + 1))
                k = slice(KD // 2 * half, KD // 2 * (half + 1))
                act.dma_start(y_out[:, k, :], x[:, k, :]).then_inc(s_out, 16)
            act.wait_ge(s_out, 32)
            for side in range(2):
                act.wait_ge(cso_free[side], 16 * (DEPTH * NXBC // 2 + 1))
            act.wait_ge(pso_free, 16 * DEPTH)
            act.wait_ge(so_free, 16 * (DEPTH * KI + 1))

        @block.vector
        def _(dve):
            dve.sem_inc(g_out, RING)
            dve.sem_inc(s_hfree, 1)
            for side in range(2):
                dve.sem_inc(cso_free[side], 16)
            dve.sem_inc(so_free, 16)
            dve.sem_inc(so_done, 1)
            dve.memset(eps[:, 0:1], EPS)
            dve.memset(eps[:, 1:2], 4 * EPS).then_inc(s_eps, 1)
            dve.memset(ztile[:, :], 0.0)
            dve.memset(xp[:, :], 0.0)
            dve.memset(ss[:, :].bitcast(F32), 1.0)
            dve.memset(lst[:, :].bitcast(F32), 1.0).then_inc(consts, 1)
            for half in range(2):
                dve.wait_ge(s_x[half], 16 * (2 - half))
                dve.sem_inc(val_in, KD // 2)

            def pcol(L, c):
                return par[:, L, bass.ds(c, 1)]

            def inverse(L, n, dst):
                dve.wait_ge(sd_done, L * N_STAT + n + 1)
                dve.reciprocal(dst[:, :], kb[0][:, 0:T])
                dve.drain()

            def clear_acc():
                dve.memset(acc[:, :], 0.0)
                dve.drain()

            def split_tile(L, k, gain, h0):
                dve.wait_ge(hi_done, L * N_HI + h0 + k + 1)
                dve.scalar_tensor_tensor(alo[:, k, :], x[:, k, :], pcol(L, gain + k), ahi[:, k, :].bitcast(F32),
                                         ALU.mult, ALU.subtract).then_inc(a_done, 1)

            def update_x(L, gain, nxt=None):
                lag = 2
                for s in range(KD + (lag if nxt else 1)):
                    if s < KD:
                        dve.scalar_tensor_tensor(t_a[:, s % RING, :], fo[:, s, :], pcol(L, gain + s), rpost[:, :], ALU.mult, ALU.mult)
                    if 1 <= s <= KD:
                        dve.tensor_tensor(x[:, s - 1, :], x[:, s - 1, :], t_a[:, (s - 1) % RING, :], ALU.add).then_inc(val_in, 1)
                    if nxt and s >= lag:
                        split_tile(L, s - lag, *nxt)
                    dve.drain()

            def ffn_in(L, ph_, h0, gt0):
                m0 = M0[ph_]
                with dve.Fori(0, KF // 2) as i:
                    for q in range(2):
                        for part in range(2):
                            r = 2 * q + part
                            dve.wait_ge(g_full, L * N_G + m0 + RING * i + r + 1)
                            dve.tensor_tensor(t_a[:, r, :], gb[r][:, 0:T], rpre[:, :], ALU.mult).then_inc(g_out, 1)
                        dve.drain()
                        dve.wait_ge(gate_done, L * N_GATE + gt0 + 2 * i + q + 1)
                        dve.tensor_tensor(t_b[:, 2 * q + 1, :], t_a[:, 2 * q + 1, :], t_b[:, 2 * q, :], ALU.mult).then_inc(val_in, 1)
                        dve.wait_ge(hi_done, L * N_HI + h0 + 2 * i + q + 1)
                        dve.tensor_tensor(blo[:, 2 * i + q, :], t_b[:, 2 * q + 1, :], bhi[:, 2 * i + q, :].bitcast(F32),
                                          ALU.subtract).then_inc(b_done, 1)

            def out_tiles(L, ph_, s0):
                clear_acc()
                with dve.Fori(0, KD // RING) as i:
                    for j in range(RING):
                        dve.wait_ge(g_full, L * N_G + M0[ph_] + RING * i + j + 1)
                        dve.tensor_copy(fo[:, RING * i + j, :], gb[j][:, 0:T]).then_inc(g_out, 1)
                        dve.wait_ge(sq_done, L * N_SQ + s0 + RING * i + j + 1)
                        dve.tensor_tensor(acc[:, :], acc[:, :], sq[:, j, :], ALU.add).then_inc(sum_done, 1)
                        dve.drain()

            def conv(L, c, m, bank, pair, side):
                dve.wait_ge(g_full, L * N_G + m + 1)
                dve.wait_ge(cso_free[side], L * (NXBC // 2 * 16) + pair * 16 + 16)
                h3 = seqs(xp[:, 0:CP], CSTRIDE)
                dve.tensor_copy(h3[:, :, 0:HIST], seqs(cst[:, c, :], HIST))
                dve.tensor_tensor(h3[:, :, HIST:CSTRIDE], seqs(gb[bank][:, 0:SAMPLE], STEPS), seqs(rpre[:, 0:SAMPLE], STEPS), ALU.mult)
                dve.tensor_tensor(xp[:, CP + HIST:CW], gb[bank][:, SAMPLE:T], rpre[:, SAMPLE:T], ALU.mult).then_inc(g_out, 1)
                dve.drain()
                dve.tensor_copy(seqs(cso[:, side, 0:SEQS * HIST], HIST), h3[:, :, STEPS:CSTRIDE])
                dve.tensor_copy(cso[:, side, SEQS * HIST:CKEEP], xp[:, CW - HIST:CW]).then_inc(cso_done, 1)
                n = CW - HIST
                dve.wait_ge(xbc_done, L * NXBC + c + 1)
                dve.tensor_scalar(cv[:, :], xp[:, 0:n], pcol(L, G_CW + CONV_K * c), None, ALU.mult)
                for k in range(1, CONV_K):
                    dve.drain()
                    ins = dve.scalar_tensor_tensor(cv[:, :], xp[:, k:k + n], pcol(L, G_CW + CONV_K * c + k), cv[:, :], ALU.mult, ALU.add)
                ins.then_inc(cv_in, 1)

            def group_b(g):
                dve.tensor_copy(bcur[:, :, :], bt[:, g, :, :]).then_inc(b_ready, 1)

            def group_b_apart(g):
                dve.tensor_tensor(bm[:, :, :], rep(bt[0:SAMPLE, g, 0, :], SEQS, 1), rep(con[0:SAMPLE, C_BLK:C_BLK + SEQS], P, 2),
                                  ALU.mult).then_inc(bm_ready, 1)

            def heads(ap, at=2):
                return rep(ap, HEAD_DIM, 3)

            def times_l(L, t, g):
                dve.wait_ge(l_exp, L * KI + t + 1)
                n0 = CHUNKS[0][1]
                l4 = lx[:, :].rearrange("p (c h i) -> p c h i", c=2, h=2)
                dve.tensor_tensor(l4, l4, rep(cb[:, g, n0:T].rearrange("p (c i) -> p c i", c=2), 2, 2), ALU.mult)
                dve.tensor_tensor(lx0[0:n0, :, :], lx0[0:n0, :, :], rep(cb[0:n0, g, 0:n0], 2, 1), ALU.mult).then_inc(m_done, 1)

            def times_dt(L, t):
                dve.wait_ge(xt_full, L * KI + t + 1)
                xt = kb[0][:, 0:3 * P].rearrange("p (c h d) -> p c h d", c=3, h=2)
                v = [b[:, :, :].rearrange("p c (h d) -> p c h d", h=2) for b in (xdt, xdec)]
                dve.tensor_tensor(v[0], xt, heads(dt[:, :, bass.ds(2 * t, 2)]), ALU.mult)
                dve.drain()
                de = dec[:, 0:DK].rearrange("p (c h) -> p c h", c=3)[:, :, bass.ds(2 * t, 2)]
                dve.tensor_tensor(v[1], v[0], heads(de), ALU.mult).then_inc(xd_done, 1)

            def ssd_step(L, t, j, g, g_next, pair, last):
                kt, q = L * KI + t, j % 2
                if not last:
                    conv(L, 2 * N_GROUPS + t + 1, M0["ssd"] + 2 * t + 1, XS_BANK, pair, 1 - q)
                dve.wait_ge(cs_full, kt + 1)
                dve.tensor_copy(pst[:, 0, :], kb[3][:, 0:P])
                dve.drain()
                for c, dst in ((1, pst[:, 1, :]), (2, pfin[:, :])):
                    for h in range(2):
                        cols = slice(h * HEAD_DIM, (h + 1) * HEAD_DIM)
                        ins = dve.scalar_tensor_tensor(dst[:, cols], pst[:, c - 1, cols], dec[:, bass.ds(DK + c * N_HEADS + 2 * t + h, 1)],
                                                       kb[3][:, c * P + h * HEAD_DIM:c * P + (h + 1) * HEAD_DIM], ALU.mult, ALU.add)
                    if c == 1:
                        dve.drain()
                ins.then_inc(p_done, 1)
                if j == TILES_PER_GROUP - 1 and not last:
                    group_b(g_next)
                if j == 0:
                    group_b_apart(g)
                if not last:
                    times_l(L, t + 1, g_next)
                z = M0["ssd"] + z_at(t, last)
                dve.wait_ge(g_full, L * N_G + z + 1)
                dve.tensor_tensor(t_b[:, 1, :], gb[Z_BANK][:, 0:T], rpre[:, :], ALU.mult).then_inc(g_out, 1)
                dve.wait_ge(e_exp, kt + 1)
                dve.wait_ge(y_full, kt + 1)
                dve.tensor_tensor(t_a[:, 0, :], kb[1][:, 0:T], eab[:, q, :], ALU.mult)
                dve.drain()
                dve.tensor_tensor(t_a[:, 1, :], kb[0][:, 0:T], t_a[:, 0, :], ALU.add).then_inc(y_read, 1)
                dve.drain()
                dve.scalar_tensor_tensor(t_a[:, 2, :], xs[:, q, :], pcol(L, G_D + t), t_a[:, 1, :], ALU.mult, ALU.add)
                dve.drain()
                dve.wait_ge(gate_done, L * N_GATE + KF + t + 1)
                dve.tensor_tensor(t_a[:, 3, :], t_a[:, 2, :], t_b[:, 0, :], ALU.mult).then_inc(val_in, 1)
                if not last:
                    times_dt(L, t + 1)
                dve.wait_ge(st_dec, kt + 1)
                dve.wait_ge(su_full, kt + 1)
                for b in range(2):
                    cols = slice(b * 4 * P, (b + 1) * 4 * P)
                    dve.tensor_tensor(so[:, cols], so[:, cols], kb[2 + b][:, :], ALU.add)
                dve.tensor_copy(so[:, SEQS * P:SO], pfin[:, :]).then_inc(so_done, 1)
                dve.wait_ge(hi_done, L * N_HI + H_Y + t + 1)
                dve.wait_ge(sq_done, L * N_SQ + S_Y + t + 1)
                dve.tensor_tensor(acc[:, :], acc[:, :], sq[:, 0, :], ALU.add)
                dve.scalar_tensor_tensor(blo[:, t, :], t_a[:, 3, :], pcol(L, G_SSD + t), bhi[:, t, :].bitcast(F32),
                                         ALU.mult, ALU.subtract).then_inc(b_done, 1)
                dve.drain()

            with dve.Fori(0, DEPTH) as L:
                for k in range(KD):
                    split_tile(L, k, G_F1A, 0)
                inverse(L, ST_F1A, rpre)
                ffn_in(L, "f1i", H_F1, 0)
                out_tiles(L, "f1o", S_F1)
                inverse(L, ST_F1B, rpost)
                update_x(L, G_F1B, (G_MA, H_X1))
                inverse(L, ST_MA, rpre)
                dve.wait_ge(g_full, L * N_G + M0["dt"] + 1)
                dve.tensor_tensor(t_a[:, 0, :], gb[0][:, 0:T], rpre[:, :], ALU.mult).then_inc(g_out, 1)
                dve.drain()
                dve.sem_inc(dt_raw, 1)

                def dt_1():
                    dve.wait_ge(dt_full, L + 1)
                    for c in range(3):
                        cols = slice(c * N_HEADS, (c + 1) * N_HEADS)
                        dve.tensor_tensor(sp[:, 0, cols], kb[1][:, c * P:c * P + N_HEADS], par[:, L, G_DTB:G_DTB + N_HEADS], ALU.add)
                    dve.drain()
                    dve.scalar_tensor_tensor(sp[:, 1, :], sp[:, 0, :], -1.0, sp[:, 0, :], ALU.mult, ALU.max).then_inc(dt_a, 1)

                def dt_2():
                    dve.wait_ge(dt_b, L * N_PBT + 1)
                    dve.tensor_scalar(sp[:, 3, :], sp[:, 2, :], 1.0, None, ALU.add).then_inc(dt_a, 1)
                    dve.drain()
                    dve.tensor_scalar(sp[:, 5, :], sp[:, 3, :], -1.0, 1e-30, ALU.add, ALU.add)
                    dve.drain()
                    dve.reciprocal(sp[:, 1, :], sp[:, 5, :])
                    dve.drain()

                def dt_3():
                    dve.wait_ge(dt_b, L * N_PBT + 2)
                    dve.tensor_scalar(sp[:, 5, :], sp[:, 4, :], 1e-30, None, ALU.add)
                    dve.drain()
                    dve.tensor_tensor(sp[:, 1, :], sp[:, 1, :], sp[:, 5, :], ALU.mult)
                    dve.drain()
                    dve.tensor_tensor(sp[:, 1, :], sp[:, 1, :], sp[:, 2, :], ALU.mult)
                    dve.drain()
                    dtf = dt[:, :, :].rearrange("p c h -> p (c h)")
                    dve.scalar_tensor_tensor(dtf, sp[:, 0, :], 0.0, sp[:, 1, :], ALU.max, ALU.add)
                    dve.drain()
                    for c in range(3):
                        ins = dve.scalar_tensor_tensor(a4[:, c, :, :], rep(dt[:, c, :], 4, 1), -1.0, rep(ea[:, :], 4, 1), ALU.mult, ALU.mult)
                    ins.then_inc(a4_done, 1)

                def rows():
                    dve.wait_ge(cum_full, L + 1)
                    cum = kb[2]
                    dve.tensor_copy(ss[0:64, :], cum[0:64, 0:T])
                    dve.tensor_copy(lst[96:128, :], cum[96:128, 0:T])
                    dve.tensor_scalar(lst[64:96, :], cum[64:96, 0:T], -1.0, None, ALU.mult)
                    dve.drain()
                    dve.tensor_tensor(ss[32:64, :], cum[32:64, 0:T], ss[32:64, :].bitcast(F32), ALU.subtract)
                    dve.tensor_tensor(lst[96:128, :], lst[96:128, :].bitcast(F32), cum[96:128, 0:T], ALU.subtract).then_inc(ss_done, 1)

                between = {0: dt_1, 1: dt_2, 2: dt_3, N_GROUPS + 2: rows}
                for c in range(2 * N_GROUPS):
                    conv(L, c, M0["bc"] + c, (1 + c) % RING, c // 2, c % 2)
                    if c in between:
                        between[c]()
                    dve.drain()
                conv(L, 2 * N_GROUPS, M0["ssd"], XS_BANK, N_GROUPS, 0)
                for g in range(N_GROUPS):
                    dve.wait_ge(cb_full, L * N_GROUPS + g + 1)
                    dve.tensor_copy(cb[:, g, :], kb[g][:, 0:T]).then_inc(cb_free, 1)
                dve.wait_ge(dec_done, L + 1)
                dve.wait_ge(bt_free, (L + 1) * N_GROUPS)
                clear_acc()
                times_l(L, 0, 0)
                times_dt(L, 0)
                per = TILES_PER_GROUP
                group_b(0)
                with dve.Fori(0, N_GROUPS - 1) as g:
                    for j in range(per):
                        ssd_step(L, per * g + j, j, g, g + (j + 1) // per, per // 2 * g + N_GROUPS + (j + 1) // 2, False)
                for j in range(per):
                    ssd_step(L, KI - per + j, j, N_GROUPS - 1, N_GROUPS - 1, (KI - per) // 2 + N_GROUPS + (j + 1) // 2, j == per - 1)
                cnt = con[:, C_CNT:C_CNT + 4 * PHIST].rearrange("p (w c) -> p w c", w=4)
                for i in range(2):
                    dve.memset(up[i][:, PP:PP + PHIST], 0.0)
                dve.drain()
                dve.wait_ge(s_ph, 16 * (L + 1))
                dve.wait_ge(so_free, 16 * (L + 1) * KI + 16)
                for k in range(KD):
                    w = k // 2
                    b = up[k % 2]
                    m = M0["mix"] + 3 * k
                    dve.wait_ge(g_full, L * N_G + m + 1)
                    h3 = seqs(b[:, 0:PP], PSTRIDE)
                    dve.tensor_copy(h3[:, :, 0:PHIST], seqs(ph[:, k, :], PHIST))
                    dve.tensor_tensor(h3[:, :, PHIST:PSTRIDE], seqs(gb[U_BANK][:, 0:SAMPLE], STEPS), seqs(rpre[:, 0:SAMPLE], STEPS), ALU.mult)
                    dve.tensor_tensor(b[:, PP + PHIST:PW], gb[U_BANK][:, SAMPLE:T], rpre[:, SAMPLE:T], ALU.mult).then_inc(g_out, 1)
                    dve.drain()
                    dve.tensor_copy(seqs(pso[:, k, 0:SEQS * PHIST], PHIST), h3[:, :, STEPS:PSTRIDE])
                    ins = dve.tensor_copy(pso[:, k, SEQS * PHIST:PKEEP], b[:, PW - PHIST:PW])
                    if k == KD - 1:
                        ins.then_inc(pso_done, 1)
                    dve.wait_ge(g_full, L * N_G + m + 2)
                    dve.tensor_tensor(t_a[:, 0, :], gb[GATE_BANK][:, 0:T], rpre[:, :], ALU.mult).then_inc(g_out, 1)
                    src, done = b, 0
                    for lvl in range(w + 1):
                        step = 1 << lvl
                        dst = win[lvl % 2]
                        dve.tensor_tensor(dst[:, done + step:PW], src[:, done + step:PW], src[:, done:PW - step], ALU.add)
                        dve.drain()
                        src, done = dst, done + step
                    p0 = PP + PHIST
                    dve.tensor_tensor(src[:, p0:p0 + PHIST], src[:, p0:p0 + PHIST], cnt[:, w, :], ALU.mult)
                    dve.drain()
                    o = pooled[:, k, :]
                    inv = 1.0 / (1 << (w + 1))
                    dve.scalar_tensor_tensor(seqs(o[:, 0:SAMPLE], STEPS), seqs(src[:, 0:PP], PSTRIDE)[:, :, PHIST:PSTRIDE], inv,
                                             h3[:, :, PHIST:PSTRIDE], ALU.mult, ALU.subtract)
                    dve.scalar_tensor_tensor(o[:, SAMPLE:T], src[:, p0:PW], inv, b[:, p0:PW], ALU.mult, ALU.subtract).then_inc(val_in, 1)
                    if k == 0:
                        inverse(L, ST_Y, rpost)
                    dve.wait_ge(g_full, L * N_G + m + 3)
                    dve.tensor_tensor(t_a[:, 1, :], gb[SB_BANK][:, 0:T], rpost[:, :], ALU.mult).then_inc(g_out, 1)
                    dve.drain()
                    dve.wait_ge(gate_done, L * N_GATE + KF + KI + k + 1)
                    dve.tensor_tensor(fo[:, k, :], t_a[:, 1, :], t_b[:, 0, :], ALU.mult)
                    dve.drain()
                for k in range(KD):
                    dve.wait_ge(hi_done, L * N_HI + H_U + k + 1)
                    dve.tensor_tensor(blo[:, k, :], pooled[:, k, :], bhi[:, k, :].bitcast(F32), ALU.subtract).then_inc(b_done, 1)
                dve.sem_inc(s_hfree, 1)
                for m in range(KD):
                    dve.wait_ge(hi_done, L * N_HI + H_PW + m + 1)
                    dve.scalar_tensor_tensor(blo[:, KD + m, :], gb[m % RING][:, 0:T], par[:, L, G_PS + m:G_PS + m + 1],
                                             bhi[:, KD + m, :].bitcast(F32), ALU.mult, ALU.subtract).then_inc(b_done, 1)
                    dve.drain()
                    dve.sem_inc(g_out, 1)
                with dve.Fori(0, KD // 2) as i:
                    for j in range(2):
                        m, r = M0["pbr"] + RING * i + 2 * j, 2 * j
                        dve.wait_ge(g_full, L * N_G + m + 1)
                        dve.tensor_tensor(t_a[:, r, :], gb[r][:, 0:T], rpre[:, :], ALU.mult).then_inc(g_out, 1)
                        dve.wait_ge(gate_done, L * N_GATE + KF + KI + KD + 2 * i + j + 1)
                        dve.wait_ge(g_full, L * N_G + m + 2)
                        dve.tensor_tensor(t_a[:, r + 1, :], gb[r + 1][:, 0:T], t_b[:, r, :], ALU.mult).then_inc(g_out, 1)
                        dve.drain()
                        dve.tensor_tensor(t_b[:, r + 1, :], t_a[:, r + 1, :], fo[:, 2 * i + j, :], ALU.add).then_inc(val_in, 1)
                        dve.wait_ge(hi_done, L * N_HI + H_MG + 2 * i + j + 1)
                        dve.tensor_tensor(blo[:, 2 * i + j, :], t_b[:, r + 1, :], bhi[:, 2 * i + j, :].bitcast(F32),
                                          ALU.subtract).then_inc(b_done, 1)
                out_tiles(L, "wo", S_WO)
                inverse(L, ST_MB, rpost)
                update_x(L, G_MB, (G_F2A, H_X2))
                dve.wait_ge(pso_free, 16 * (L + 1))
                inverse(L, ST_F2A, rpre)
                ffn_in(L, "f2i", H_F2, KF + KI + 2 * KD)
                out_tiles(L, "f2o", S_F2)
                inverse(L, ST_F2B, rpost)
                update_x(L, G_F2B)

        @block.tensor
        def _(pe):
            pe.sem_inc(w_free, RING - 1)

            def unit(L, u, slot, bank, hi, lo, k0, first, last, tiles=UT, w0=0, fresh=True, behind=None):
                if fresh:
                    pe.wait_ge(w_lo, L * UNITS + u + 1)
                for j in range(tiles):
                    w = slice((w0 + j) * P, (w0 + j + 1) * P)
                    xh, xl = hi[:, k0 + j, :], lo[:, k0 + j, :]
                    ins = pe.matmul(gb[bank][:, 0:T], whi[:, slot, w], xh, start=first and j == 0, stop=False)
                    if fresh and j == 0:
                        ins.then_inc(w_free, 1)
                    pe.matmul(gb[bank][:, 0:T], whi[:, slot, w], xl, start=False, stop=False)
                    ins = pe.matmul(gb[bank][:, 0:T], wlo[:, slot, w], xh, start=False, stop=last and j == tiles - 1)
                    if last and j == tiles - 1:
                        ins.then_inc(g_full, 1)
                    if behind:
                        behind(j)

            def room(L, m, back=RING):
                pe.wait_ge(g_out, L * N_G + m + 1 + RING - back)

            def from_a(L, u, slot, m, bank):
                room(L, m)
                unit(L, u, slot, bank, ahi, alo, 0, True, True)

            def mean(L, n):
                pe.wait_ge(consts, 2)
                pe.matmul(kb[0][:, 0:T], cc(C_ONE), acc[:, :], start=True, stop=True).then_inc(stat_full, 1)

            def first_units(L, phase, a0, n, stat):
                u, m = U0[phase], M0[phase]
                late = 2
                for k in range(KD + late):
                    if k < KD:
                        pe.wait_ge(a_done, L * N_A + a0 + k + 1)
                    if k == KD - 2:
                        pe.wait_ge(x_sum, L * N_XSUM + (n + 1) * (KD - 1))
                        mean(L, stat)
                    for s in range(RING):
                        j = k - late if s == RING - 1 else k
                        if not 0 <= j < KD:
                            continue
                        if j == 0:
                            pe.wait_ge(w_lo, L * UNITS + u + s + 1)
                            room(L, m + s)
                        w = slice(j * P, (j + 1) * P)
                        ins = pe.matmul(gb[s][:, 0:T], whi[:, s, w], ahi[:, j, :], start=j == 0, stop=False)
                        if (s, j) == (0, 0) or (s in (1, 2) and j == KD - 1) or (s == 3 and j == KD - 1):
                            ins.then_inc(w_free, 1)
                        pe.matmul(gb[s][:, 0:T], whi[:, s, w], alo[:, j, :], start=False, stop=False)
                        ins = pe.matmul(gb[s][:, 0:T], wlo[:, s, w], ahi[:, j, :], start=False, stop=j == KD - 1)
                        if j == KD - 1:
                            ins.then_inc(g_full, 1)

            def ffn(L, p, a0, b0, n, n_in, n_out):
                first_units(L, p + "i", a0, n, n_in)
                with pe.Fori(1, KF // 2) as i:
                    for s in range(RING):
                        from_a(L, U0[p + "i"] + RING * i + s, s, M0[p + "i"] + RING * i + s, s)
                with pe.Fori(0, KD // RING) as i:
                    for j in range(RING):
                        room(L, M0[p + "o"] + RING * i + j)
                        for s in range(OUT_UNITS):
                            c = OUT_UNITS * j + s
                            pe.wait_ge(b_done, L * N_B + b0 + min(KF, UT * (s + 1)))
                            unit(L, U0[p + "o"] + OUT_UNITS * RING * i + c, c % RING, j, bhi, blo, UT * s, s == 0, s == OUT_UNITS - 1,
                                 min(UT, KF - UT * s))
                pe.wait_ge(sum_done, L * N_SUM + (3 if p == "f2" else 1) * KD)
                mean(L, n_out)

            def log_l(L, t):
                n0 = CHUNKS[0][1]
                pe.wait_ge(rx_done, L * KI + t + 1)
                for c in (1, 2):
                    c0, n = CHUNKS[c]
                    dst = gb[2][:, (c - 1) * 2 * P:c * 2 * P]
                    pe.matmul(dst, lst[:, c0:c0 + n], rx[:, :, c0:c0 + n], start=True, stop=False)
                    pe.matmul(dst, identr[:, :], rep(maskr[:, 0:P], 2, 1), start=False, stop=True)
                dst = gb[3][0:n0, 0:2 * n0]
                pe.matmul(dst, lst[:, 0:n0], rx[:, :, 0:n0], start=True, stop=False)
                pe.matmul(dst, identr[0:n0, 0:n0], rep(maskr[0:n0, P:P + n0], 2, 1), start=False, stop=True)
                for h in range(2):
                    ins = pe.matmul(gb[3][:, 2 * n0:2 * n0 + T], halfr[:, h * P:(h + 1) * P], rx[0:HEAD_DIM, h, :], start=h == 0, stop=h == 1)
                ins.then_inc(l_full, 1)

            def x_token_major(L, t, q):
                pe.wait_ge(xbc_done, L * NXBC + 2 * N_GROUPS + t + 2)
                for c, (c0, n) in enumerate(CHUNKS):
                    ins = pe.transpose(kb[0][:, c * P:(c + 1) * P], xs[:, q, c0:c0 + P], cc(C_ID))
                ins.then_inc(xt_full, 1)

            def ssd_step(L, t, q, g, first, last):
                kt = L * KI + t
                n0 = CHUNKS[0][1]
                if not last:
                    pe.wait_ge(g_out, L * N_G + M0["ssd"] + 2 * t + 1 + RING)
                    unit(L, U0["ssd"] + 2 * t + 1, slot_of("ssd", 2 * q + 1), XS_BANK, ahi, alo, 0, True, True)
                pe.wait_ge(xd_done, kt + 1)
                pe.wait_ge(so_done, kt + 1)
                if first:
                    pe.wait_ge(b_ready, L * N_GROUPS + g + 1)
                for c, rows in ((0, slice(SAMPLE, n0)), (1, slice(0, P)), (2, slice(0, P))):
                    ins = pe.matmul(kb[3][:, c * P:(c + 1) * P], bcur[rows, c, :], xdec[rows, c, :], start=True, stop=True)
                ins.then_inc(cs_full, 1)
                pe.wait_ge(m_done, kt + 1)
                for h in range(2):
                    ch = slice(h * HEAD_DIM, (h + 1) * HEAD_DIM)
                    for c, (c0, n) in enumerate(CHUNKS):
                        rhs = lx0[0:n0, h, :] if c == 0 else lx[:, ((c - 1) * 2 + h) * P:((c - 1) * 2 + h + 1) * P]
                        pe.matmul(kb[0][ch, c0:c0 + n], xdt[0:n, c, ch], rhs, start=True, stop=True)
                if not last:
                    pe.wait_ge(e_exp, kt + 1)
                    log_l(L, t + 1)
                if last:
                    pe.wait_ge(g_out, L * N_G + M0["ssd"] + 2 * t + 1 + RING)
                pe.wait_ge(st_landed, 16 * (L * KI + t) + 16)
                cg = N_GROUPS + g

                def from_state(b):
                    c = slice(b * STEPS, (b + 1) * STEPS)
                    pe.matmul(kb[1][:, c], st[:, b * P:(b + 1) * P], bc[:, cg, c], start=True, stop=True)
                    if b == SEQS - 1:
                        pe.matmul(kb[1][:, SAMPLE:n0], ztile[:, :], bc[:, cg, SAMPLE:n0], start=True, stop=True)

                unit(L, U0["ssd"] + z_at(t, last), slot_of("ssd", z_at(q + 2, last)), Z_BANK, ahi, alo, 0, True, True, behind=from_state)
                pe.wait_ge(p_done, kt + 1)
                for c in (1, 2):
                    c0, n = CHUNKS[c]
                    ins = pe.matmul(kb[1][:, c0:c0 + n], pst[:, c - 1, :], bc[:, cg, c0:c0 + n], start=True, stop=True)
                ins.then_inc(y_full, 1)
                if first:
                    pe.wait_ge(bm_ready, L * N_GROUPS + g + 1)
                for b in range(SEQS):
                    ins = pe.matmul(kb[2 + b // 4][:, (b % 4) * P:(b % 4 + 1) * P], bm[:, b, :], xdec[0:SAMPLE, 0, :], start=True, stop=True)
                ins.then_inc(su_full, 1)
                if not last:
                    pe.wait_ge(y_read, kt + 1)
                    x_token_major(L, t + 1, 1 - q)

            with pe.Fori(0, DEPTH) as L:
                ffn(L, "f1", 0, 0, 0, ST_F1A, ST_F1B)
                first_units(L, "dt", KD, 1, ST_MA)

                def from_bc(c):
                    from_a(L, U0["bc"] + c, slot_of("bc", c), M0["bc"] + c, (1 + c) % RING)

                def b_token_major(g):
                    pe.wait_ge(xbc_done, L * NXBC + g + 2)
                    if g >= 2:
                        pe.wait_ge(bt_free, L * N_GROUPS + g - 1)
                    for c, (c0, n) in enumerate(CHUNKS):
                        ins = pe.transpose(kb[g % 2][:, c * P:(c + 1) * P], bc[:, g, c0:c0 + P], cc(C_ID))
                    ins.then_inc(bt_full, 1)

                for c in range(N_GROUPS - 1, N_GROUPS + 2):
                    from_bc(c)
                    if c == N_GROUPS - 1:
                        pe.wait_ge(dt_raw, L + 1)
                        for k, (c0, n) in enumerate(CHUNKS):
                            ins = pe.transpose(kb[1][:, k * P:(k + 1) * P], t_a[:, 0, c0:c0 + P], cc(C_ID))
                        ins.then_inc(dt_full, 1)
                b_token_major(0)
                from_bc(N_GROUPS + 2)
                pe.wait_ge(a4_done, L + 1)
                for c, (c0, n) in enumerate(CHUNKS):
                    pe.matmul(kb[2][:, c0:c0 + n], a4[0:n, c, :, :].rearrange("p r h -> p (r h)"), cc(tri(c), n, n), start=True, stop=True)
                    pe.matmul(kb[3][:, c * N_HEADS:(c + 1) * N_HEADS], cc(C_LAT0 if c == 0 else C_LAT1, P, n), a4[0:n, c, 0, :], start=True, stop=True)
                    pe.matmul(kb[3][:, DK + c * N_HEADS:DK + (c + 1) * N_HEADS], cc(C_META if c == 0 else C_ONE, P, n), a4[0:n, c, 0, :], start=True, stop=True)
                for b in range(SEQS):
                    ins = pe.matmul(kb[3][:, 2 * DK + b * N_HEADS:2 * DK + (b + 1) * N_HEADS], con[0:SAMPLE, C_BLK + b:C_BLK + b + 1].broadcast_to([SAMPLE, P]),
                                    a4[0:SAMPLE, 0, 0, :], start=True, stop=True)
                ins.then_inc(cum_full, 1)
                b_token_major(1)
                from_bc(N_GROUPS + 3)
                b_token_major(2)
                from_a(L, U0["ssd"], slot_of("ssd", 0), M0["ssd"], XS_BANK)
                b_token_major(3)
                pe.wait_ge(ss_done, L + 1)
                pe.wait_ge(dec_done, L + 1)
                for g in range(N_GROUPS):
                    pe.wait_ge(xbc_done, L * NXBC + N_GROUPS + g + 2)
                    if g < 2:
                        pe.wait_ge(bt_free, L * N_GROUPS + g + 3)
                    for c, (c0, n) in enumerate(CHUNKS):
                        ins = pe.matmul(kb[g][:, c0:c0 + n], bc[:, g, c0:c0 + P], bc[:, N_GROUPS + g, c0:c0 + n], start=True, stop=True)
                    ins.then_inc(cb_full, 1)
                pe.wait_ge(cb_free, (L + 1) * N_GROUPS)
                log_l(L, 0)
                x_token_major(L, 0, 0)
                per = TILES_PER_GROUP
                with pe.Fori(0, N_GROUPS - 1) as g:
                    for j in range(per):
                        ssd_step(L, per * g + j, j % 2, g, j == 0, False)
                for j in range(per):
                    ssd_step(L, KI - per + j, j % 2, N_GROUPS - 1, j == 0, j == per - 1)

                def mix(k, first):
                    for n, bank in ((0, U_BANK), (1, GATE_BANK)):
                        room(L, M0["mix"] + 3 * k + n, 3)
                        unit(L, U0["mix"] + 4 * k + n, slot_of("mix", n), bank, ahi, alo, 0, True, True)
                    if first:
                        pe.wait_ge(b_done, L * N_B + KF + KI)
                        mean(L, ST_Y)
                    room(L, M0["mix"] + 3 * k + 2, 3)
                    for n in range(2):
                        unit(L, U0["mix"] + 4 * k + 2 + n, slot_of("mix", 2 + n), SB_BANK, bhi, blo, UT * n, n == 0, n == 1)

                mix(0, True)
                with pe.Fori(1, KD) as k:
                    mix(k, False)
                g = 0
                for n, groups in enumerate(PW_UNITS):
                    for h in range(groups):
                        pe.wait_ge(b_done, L * N_B + KF + KI + 2 * (g + 1))
                        for mm in range(2):
                            m = 2 * g + mm
                            room(L, M0["pw"] + m)
                            unit(L, U0["pw"] + n, slot_of("pw", n), m % RING, bhi, blo, 2 * g, True, True, 2, 4 * h + 2 * mm, h == mm == 0)
                        g += 1
                with pe.Fori(0, KD // 2) as i:
                    for j in range(2):
                        from_a(L, U0["pbr"] + RING * i + 2 * j, 2 * j, M0["pbr"] + RING * i + 2 * j, 2 * j)
                        room(L, M0["pbr"] + RING * i + 2 * j + 1)
                        pe.wait_ge(b_done, L * N_B + KF + KI + 2 * KD)
                        unit(L, U0["pbr"] + RING * i + 2 * j + 1, 2 * j + 1, 2 * j + 1, bhi, blo, KD, True, True)
                with pe.Fori(0, KD // RING) as i:
                    for s in range(RING):
                        pe.wait_ge(b_done, L * N_B + KF + KI + 3 * KD - 1)

                        def last_tile(k):
                            if s == 0 and k == KD - 2:
                                pe.wait_ge(b_done, L * N_B + KF + KI + 3 * KD)

                        room(L, M0["wo"] + RING * i + s)
                        unit(L, U0["wo"] + RING * i + s, s, s, bhi, blo, 0, True, True, behind=last_tile)
                pe.wait_ge(sum_done, L * N_SUM + 2 * KD)
                mean(L, ST_MB)
                ffn(L, "f2", 2 * KD, KF + KI + 3 * KD, 2, ST_F2A, ST_F2B)


def kernel(**inputs):
    import numpy as np
    import concourse.bacc as bacc
    from concourse.bass_utils import run_bass_kernel_spmd

    f = {k: np.ascontiguousarray(v) for k, v in inputs.items()}

    def tiles(w):
        d, k, m = w.shape
        return w.reshape(d, k // P, P, m // P, P).transpose(0, 1, 3, 2, 4)

    wts = np.zeros((DEPTH, UNITS, UT, P, P), np.float32)
    zxbc = np.ascontiguousarray(f["w_in"][:, :, :D_INNER + (KI + 2 * N_GROUPS) * P])
    rest = np.ascontiguousarray(f["w_in"][:, :, D_INNER + NXBC * P + N_HEADS:])
    zx, ug = tiles(zxbc), tiles(rest)
    for p, n in (("f1", "ffn1"), ("f2", "ffn2")):
        wi, wo = tiles(f[n + "_w_in"]), tiles(f[n + "_w_out"])
        for j in range(KF):
            wts[:, U0[p + "i"] + 2 * j] = wi[:, :, j]
            wts[:, U0[p + "i"] + 2 * j + 1] = wi[:, :, KF + j]
        for m in range(KD):
            for s in range(OUT_UNITS):
                part = wo[:, UT * s:UT * (s + 1), m]
                wts[:, U0[p + "o"] + OUT_UNITS * m + s, :part.shape[1]] = part
    for c in range(2 * N_GROUPS):
        wts[:, U0["bc"] + c] = zx[:, :, 2 * KI + c]
    for t in range(KI):
        wts[:, U0["ssd"] + (2 * t - 1 if t else 0)] = zx[:, :, KI + t]
        wts[:, U0["ssd"] + z_at(t, t == KI - 1)] = zx[:, :, t]
    at = D_INNER + NXBC * P
    wts[:, U0["dt"], :, :, :N_HEADS] = f["w_in"][:, :, at:at + N_HEADS].reshape(DEPTH, KD, P, N_HEADS)
    sbr, pbr, wo = tiles(f["w_ssd_branch"]), tiles(f["w_pool_branch"]), tiles(f["w_out"])
    for m in range(KD):
        wts[:, U0["mix"] + 4 * m] = ug[:, :, m]
        wts[:, U0["mix"] + 4 * m + 1] = ug[:, :, KD + m]
        wts[:, U0["mix"] + 4 * m + 2] = sbr[:, :UT, m]
        wts[:, U0["mix"] + 4 * m + 3] = sbr[:, UT:, m]
        wts[:, U0["pbr"] + 2 * m] = ug[:, :, 2 * KD + m]
        wts[:, U0["pbr"] + 2 * m + 1] = pbr[:, :, m]
        wts[:, U0["wo"] + m] = wo[:, :, m]
    g = 0
    for n, groups in enumerate(PW_UNITS):
        for h in range(groups):
            pw = tiles(f["pool_w"][:, g])
            for mm in range(2):
                wts[:, U0["pw"] + n, 4 * h + 2 * mm:4 * h + 2 * mm + 2] = pw[:, :, mm]
            g += 1
    wts = np.ascontiguousarray(wts.transpose(0, 1, 3, 2, 4)).reshape(DEPTH * UNITS, P, UT * P)

    def cols(v, n):
        return v.reshape(DEPTH, n, P).transpose(2, 0, 1)

    def conv_order(v):
        return np.concatenate([v[..., D_INNER:], v[..., :D_INNER]], axis=-1)

    par = np.zeros((P, DEPTH, NPAR), np.float32)
    for at, n in ((G_F1A, "ln_ffn1_pre"), (G_F1B, "ln_ffn1_post"), (G_MA, "ln_mix_pre"), (G_MB, "ln_mix_post"),
                  (G_F2A, "ln_ffn2_pre"), (G_F2B, "ln_ffn2_post"), (G_PS, "pool_scale")):
        par[:, :, at:at + KD] = cols(f[n], KD)
    par[:, :, G_SSD:G_SSD + KI] = cols(f["ssd_norm"], KI)
    par[:, :, G_D:G_D + KI] = cols(np.repeat(f["d_skip"], HEAD_DIM, axis=1), KI)
    par[:, :, G_CB:G_CB + NXBC] = cols(conv_order(f["conv_b"]), NXBC)
    for k in range(CONV_K):
        par[:, :, G_CW + k:G_CW + CONV_K * NXBC:CONV_K] = cols(conv_order(f["conv_w"][:, k]), NXBC)
    par[:, :, G_DTB:G_DTB + N_HEADS] = f["dt_bias"][None]
    par[:, :, G_AL:G_AL + N_HEADS] = f["a_log"][None]

    con = np.zeros((P, NCON), np.float32)
    ar = np.arange(P)
    seq = np.where(ar < SAMPLE, ar // STEPS, SEQS)
    same = seq[:, None] == seq[None, :]
    before = ar[:, None] <= ar[None, :]
    real = (ar < CHUNKS[0][1])
    con[:, C_ID:C_ID + P] = np.eye(P)
    con[:, C_TRI1:C_TRI1 + P] = before
    con[:, C_TRI0:C_TRI0 + P] = before & same
    con[:, C_LAT1:C_LAT1 + P] = ~before
    con[:, C_LAT0:C_LAT0 + P] = ~before & same & real[None, :]
    con[:, C_ONE:C_ONE + P] = 1
    con[SAMPLE:CHUNKS[0][1], C_META:C_META + P] = 1
    own = np.zeros((P, 4 * P), np.float32)
    own[:, 0:P] = np.where(before, 0, MASKED)
    own[:, P:2 * P] = np.where(before & same, 0, MASKED)
    own[:, 2 * P:2 * P + HEAD_DIM] = 1
    own[:, 3 * P + HEAD_DIM:] = 1
    con[:, C_SEL:C_SEL + N_HEADS] = (ar % N_HEADS)[:, None] == np.arange(N_HEADS)
    con[:SAMPLE, C_BLK:C_BLK + SEQS] = (ar[:SAMPLE] // STEPS)[:, None] == np.arange(SEQS)
    for w in range(4):
        win = 2 << w
        con[:, C_CNT + w * PHIST:C_CNT + (w + 1) * PHIST] = win / np.minimum(np.arange(PHIST) + 1, win)

    tokens = np.concatenate([f["x_sample"].reshape(SAMPLE, D_MODEL), f["meta_tokens"], f["x_prompt"][0]])
    arrays = {
        "x_in": tokens.T.reshape(KD, P, T).transpose(1, 0, 2),
        "wts": wts,
        "par_in": par,
        "con_in": con,
        "own_dram": own,
        "cst_in": conv_order(f["state_conv"]).reshape(DEPTH, SEQS * HIST, NXBC, P).transpose(0, 3, 2, 1),
        "pst_in": f["state_pool"].reshape(DEPTH, SEQS * PHIST, KD, P).transpose(0, 3, 2, 1),
        "ssm_in": f["state_ssm"].reshape(DEPTH, SEQS, KI, P, D_STATE).transpose(0, 2, 4, 1, 3).reshape(DEPTH * KI, P, SEQS * P),
    }
    outs = {"y": (P, KD, T), "ssm_o": (DEPTH * KI, P, SO), "conv_o": (DEPTH * NXBC, P, CKEEP), "pool_o": (DEPTH, P, KD, PKEEP)}
    nc = bacc.Bacc("TRN2", target_bir_lowering=False, num_devices=1)
    arrays = {k: np.ascontiguousarray(v) for k, v in arrays.items()}
    aps = [nc.dram_tensor(k, v.shape, F32, kind="ExternalInput").ap() for k, v in arrays.items()]
    aps += [nc.dram_tensor(k, s, F32, kind="ExternalOutput").ap() for k, s in outs.items()]
    build(nc, *aps)
    got = run_bass_kernel_spmd(nc, [arrays], core_ids=[0]).results[0]

    y = got["y"].transpose(1, 0, 2).reshape(D_MODEL, T).T
    s = got["ssm_o"].reshape(DEPTH, KI, D_STATE, SEQS + 1, P).transpose(3, 0, 1, 4, 2).reshape(SEQS + 1, DEPTH, N_HEADS, HEAD_DIM, D_STATE)
    c = got["conv_o"].reshape(DEPTH, NXBC * P, SEQS + 1, HIST).transpose(0, 2, 3, 1)
    c = np.concatenate([c[..., 2 * N_GROUPS * P:], c[..., :2 * N_GROUPS * P]], axis=-1)
    p = got["pool_o"].transpose(0, 2, 1, 3).reshape(DEPTH, D_MODEL, SEQS + 1, PHIST).transpose(0, 2, 3, 1)
    return tuple(np.ascontiguousarray(v) for v in (
        y[SAMPLE + N_META:].reshape(1, SEQ, D_MODEL), y[:SAMPLE].reshape(SEQS, STEPS, D_MODEL),
        s[SEQS:].transpose(1, 0, 2, 3, 4), c[:, SEQS:], p[:, SEQS:],
        s[:SEQS].transpose(1, 0, 2, 3, 4), c[:, :SEQS], p[:, :SEQS]))
```
